# Optimizing a Trainium2 kernel written in Bass

```python
import jax, jax.numpy as jnp
from jax import lax
import numpy as np

D_MODEL = 2048
BATCH = 1
SEQ = 256
DEPTH = 2

MIX_WIDTH = D_MODEL
RWKV_WIDTH = MIX_WIDTH // 2
RWKV_HEAD = 64
RWKV_HEADS = RWKV_WIDTH // RWKV_HEAD
DECAY_LORA = 64
ICLR_LORA = 64
VRES_LORA = 32
GATE_LORA = 128
ATTN_WIDTH = MIX_WIDTH - RWKV_WIDTH
ATTN_HEAD = 128
ATTN_HEADS = ATTN_WIDTH // ATTN_HEAD
MOBA_BLOCK = 256
MOBA_TOPK = 3
QUERY_CHUNK = 16
ROPE_THETA = 10000.0
D_FF = 4 * D_MODEL
NORM_EPS = 1e-6
LNX_EPS = 64e-5
N_SHIFT = 3 * RWKV_WIDTH + DECAY_LORA + ICLR_LORA + GATE_LORA
N_IN = N_SHIFT + 3 * ATTN_WIDTH

kernel_name = 'hybrid_rwkv7_moba_sandwich'

def rms_norm(x, gain):
    xf = x.astype(jnp.float32)
    y = xf * lax.rsqrt(jnp.mean(xf * xf, axis=-1, keepdims=True) + NORM_EPS)
    return (y * gain.astype(jnp.float32)).astype(x.dtype)

def token_shift(z, mu):
    prev = jnp.pad(z[:, :-1], ((0, 0), (1, 0), (0, 0)))
    return z + (prev - z) * mu

def wkv7_scan(r, w, k, v, a, b):
    bsz, _, nh, n = r.shape

    def step(state, inp):
        r_t, w_t, k_t, v_t, a_t, b_t = inp
        sa = jnp.einsum('bhij,bhj->bhi', state, a_t)
        state = (state * w_t[:, :, None, :] + sa[..., None] * b_t[:, :, None, :]
                 + v_t[..., None] * k_t[:, :, None, :])
        return state, jnp.einsum('bhij,bhj->bhi', state, r_t)

    xs = tuple(jnp.moveaxis(t, 1, 0) for t in (r, w, k, v, a, b))
    state0 = jnp.zeros((bsz, nh, n, n), jnp.float32)
    _, y = lax.scan(step, state0, xs)
    return jnp.moveaxis(y, 0, 1)

def rwkv7_mix(zs, v_first, vres, w0, w2, a0, a2, g2, k_k, k_a, r_k, lnx_g, lnx_b):
    bsz, s, _ = zs.shape
    c = RWKV_WIDTH
    f32 = jnp.float32
    r, k, v = zs[..., :c], zs[..., c:2 * c], zs[..., 2 * c:3 * c]
    o = 3 * c
    wd = zs[..., o:o + DECAY_LORA]
    o += DECAY_LORA
    ad = zs[..., o:o + ICLR_LORA]
    o += ICLR_LORA
    gd = zs[..., o:o + GATE_LORA]
    w_log = -jax.nn.softplus(-(w0 + jnp.tanh(wd) @ w2)) - 0.5
    decay = jnp.exp(-jnp.exp(w_log.astype(f32)))
    a = jax.nn.sigmoid(a0 + ad @ a2)
    g = jax.nn.sigmoid(gd) @ g2
    if vres is not None:
        vd, v0, v2 = vres
        v = v + (v_first - v) * jax.nn.sigmoid(v0 + vd @ v2)
    heads = lambda t: t.reshape(bsz, s, RWKV_HEADS, RWKV_HEAD).astype(f32)
    kk = heads(k * k_k)
    kk = kk / jnp.maximum(jnp.sqrt(jnp.sum(kk * kk, axis=-1, keepdims=True)), 1e-12)
    k = k * (1 + (a - 1) * k_a)
    rh, kh, vh, ah = heads(r), heads(k), heads(v), heads(a)
    y = wkv7_scan(rh, heads(decay), kh, vh, -kk, kk * ah)
    mu = jnp.mean(y, axis=-1, keepdims=True)
    var = jnp.mean(jnp.square(y - mu), axis=-1, keepdims=True)
    yn = ((y - mu) * lax.rsqrt(var + LNX_EPS)).reshape(bsz, s, c)
    yn = yn * lnx_g.astype(f32) + lnx_b.astype(f32)
    bonus = jnp.sum(rh * kh * r_k.astype(f32), axis=-1, keepdims=True) * vh
    out = (yn + bonus.reshape(bsz, s, c)) * g.astype(f32)
    return out.astype(zs.dtype), v

def rope(x, positions):
    half = x.shape[-1] // 2
    inv_freq = ROPE_THETA ** (-jnp.arange(half, dtype=jnp.float32) / half)
    ang = positions.astype(jnp.float32)[:, None] * inv_freq[None, :]
    cos, sin = jnp.cos(ang), jnp.sin(ang)
    xf = x.astype(jnp.float32)
    x1, x2 = xf[..., :half], xf[..., half:]
    return jnp.concatenate([x1 * cos - x2 * sin, x2 * cos + x1 * sin], axis=-1).astype(x.dtype)

def moba_attention(q, k, v):
    bsz, nh, s, dh = q.shape
    f32 = jnp.float32
    nb = -(-s // MOBA_BLOCK)
    s_pad = nb * MOBA_BLOCK
    pad = ((0, 0), (0, 0), (0, s_pad - s), (0, 0))
    q, k, v = (jnp.pad(t, pad) for t in (q, k, v))
    k_blk = k.reshape(bsz, nh, nb, MOBA_BLOCK, dh).astype(f32)
    v_blk = v.reshape(bsz, nh, nb, MOBA_BLOCK, dh).astype(f32)
    k_mean = jnp.mean(k_blk, axis=3)
    gate = jnp.einsum('bhsd,bhnd->bhsn', q.astype(f32), k_mean)
    q_blk = jnp.arange(s_pad) // MOBA_BLOCK
    past = jnp.arange(nb)[None, :] < q_blk[:, None]
    gate = jnp.where(past, gate, -jnp.inf)
    topk = min(MOBA_TOPK, nb)
    sel_score, sel_idx = lax.top_k(gate, topk)
    sel_valid = jnp.isfinite(sel_score)

    n_chunks = s_pad // QUERY_CHUNK
    scale = dh ** -0.5

    def to_chunks(t):
        t = t.reshape(bsz, nh, n_chunks, QUERY_CHUNK, *t.shape[3:])
        return jnp.moveaxis(t, 2, 0)

    b_idx = jnp.arange(bsz)[:, None, None, None]
    h_idx = jnp.arange(nh)[None, :, None, None]
    q_offs = jnp.arange(QUERY_CHUNK)
    k_offs = jnp.arange(MOBA_BLOCK)

    def attend(inp):
        c, q_c, idx_c, valid_c = inp
        start = c * QUERY_CHUNK
        own = start // MOBA_BLOCK
        k_sel = k_blk[b_idx, h_idx, idx_c]
        v_sel = v_blk[b_idx, h_idx, idx_c]
        k_own = lax.dynamic_index_in_dim(k_blk, own, axis=2, keepdims=False)
        v_own = lax.dynamic_index_in_dim(v_blk, own, axis=2, keepdims=False)
        qf = q_c.astype(f32) * scale
        s_sel = jnp.einsum('bhqd,bhqkjd->bhqkj', qf, k_sel)
        s_sel = jnp.where(valid_c[..., None], s_sel, -jnp.inf)
        s_sel = s_sel.reshape(bsz, nh, QUERY_CHUNK, topk * MOBA_BLOCK)
        s_own = jnp.einsum('bhqd,bhjd->bhqj', qf, k_own)
        q_pos = start + q_offs
        k_pos = own * MOBA_BLOCK + k_offs
        s_own = jnp.where(k_pos[None, :] <= q_pos[:, None], s_own, -jnp.inf)
        p = jax.nn.softmax(jnp.concatenate([s_sel, s_own], axis=-1), axis=-1)
        p_sel = p[..., :topk * MOBA_BLOCK].reshape(bsz, nh, QUERY_CHUNK, topk, MOBA_BLOCK)
        p_own = p[..., topk * MOBA_BLOCK:]
        o = (jnp.einsum('bhqkj,bhqkjd->bhqd', p_sel, v_sel)
             + jnp.einsum('bhqj,bhjd->bhqd', p_own, v_own))
        return o.astype(q_c.dtype)

    out = lax.map(attend, (jnp.arange(n_chunks), to_chunks(q), to_chunks(sel_idx), to_chunks(sel_valid)))
    out = jnp.moveaxis(out, 0, 2).reshape(bsz, nh, s_pad, dh)
    return out[:, :, :s]

def setup_inputs(seed: int = 0) -> dict:
    key = jax.random.key(seed)
    ks = iter(jax.random.split(key, 32))
    nrm = lambda shape, scale: jax.random.normal(next(ks), shape, jnp.float32) * scale
    gain = lambda shape: 1.0 + nrm(shape, 0.05)
    unif = lambda shape: jax.random.uniform(next(ks), shape, jnp.float32)
    L, Lv, C = DEPTH, DEPTH - 1, RWKV_WIDTH
    return {
        'x': nrm((BATCH, SEQ, D_MODEL), 1.0),
        'norm_mix_pre': gain((L, D_MODEL)),
        'norm_mix_post': gain((L, D_MODEL)),
        'norm_mlp_pre': gain((L, D_MODEL)),
        'norm_mlp_post': gain((L, D_MODEL)),
        'w_in': nrm((L, D_MODEL, N_IN), D_MODEL ** -0.5),
        'w_in_vres': nrm((Lv, D_MODEL, VRES_LORA), D_MODEL ** -0.5),
        'shift_mu': unif((L, N_SHIFT)),
        'shift_mu_vres': unif((Lv, VRES_LORA)),
        'decay_w0': nrm((L, C), 0.5),
        'decay_w2': nrm((L, DECAY_LORA, C), 0.5 * DECAY_LORA ** -0.5),
        'iclr_a0': nrm((L, C), 0.5),
        'iclr_a2': nrm((L, ICLR_LORA, C), 0.5 * ICLR_LORA ** -0.5),
        'vres_v0': nrm((Lv, C), 0.5),
        'vres_v2': nrm((Lv, VRES_LORA, C), 0.5 * VRES_LORA ** -0.5),
        'gate_g2': nrm((L, GATE_LORA, C), GATE_LORA ** -0.5),
        'k_k': 0.85 + nrm((L, C), 0.05),
        'k_a': gain((L, C)),
        'r_k': nrm((L, RWKV_HEADS, RWKV_HEAD), 0.1),
        'lnx_gain': gain((L, C)),
        'lnx_bias': nrm((L, C), 0.01),
        'w_out': nrm((L, MIX_WIDTH, D_MODEL), MIX_WIDTH ** -0.5),
        'w_up': nrm((L, D_MODEL, D_FF), D_MODEL ** -0.5),
        'w_down': nrm((L, D_FF, D_MODEL), D_FF ** -0.5),
    }

def reference(x, norm_mix_pre, norm_mix_post, norm_mlp_pre, norm_mlp_post, w_in, w_in_vres,
              shift_mu, shift_mu_vres, decay_w0, decay_w2, iclr_a0, iclr_a2, vres_v0, vres_v2,
              gate_g2, k_k, k_a, r_k, lnx_gain, lnx_bias, w_out, w_up, w_down):
    bsz, s, _ = x.shape
    positions = jnp.arange(s)
    v_first = None
    for i in range(DEPTH):
        h = rms_norm(x, norm_mix_pre[i])
        w_comb = w_in[i] if i == 0 else jnp.concatenate([w_in[i], w_in_vres[i - 1]], axis=1)
        z = h @ w_comb
        z_rwkv = token_shift(z[..., :N_SHIFT], shift_mu[i])
        z_att = z[..., N_SHIFT:N_IN]
        vres = None if i == 0 else (token_shift(z[..., N_IN:], shift_mu_vres[i - 1]),
                                    vres_v0[i - 1], vres_v2[i - 1])
        y_r, v_r = rwkv7_mix(z_rwkv, v_first, vres, decay_w0[i], decay_w2[i], iclr_a0[i], iclr_a2[i],
                             gate_g2[i], k_k[i], k_a[i], r_k[i], lnx_gain[i], lnx_bias[i])
        if i == 0:
            v_first = v_r
        qkv = z_att.reshape(bsz, s, 3, ATTN_HEADS, ATTN_HEAD)
        q = rope(jnp.transpose(qkv[:, :, 0], (0, 2, 1, 3)), positions)
        k = rope(jnp.transpose(qkv[:, :, 1], (0, 2, 1, 3)), positions)
        v = jnp.transpose(qkv[:, :, 2], (0, 2, 1, 3))
        y_a = jnp.transpose(moba_attention(q, k, v), (0, 2, 1, 3)).reshape(bsz, s, ATTN_WIDTH)
        y = jnp.concatenate([y_r, y_a], axis=-1) @ w_out[i]
        x = x + rms_norm(y, norm_mix_post[i])
        h = rms_norm(x, norm_mlp_pre[i])
        m = jnp.square(jax.nn.relu(h @ w_up[i])) @ w_down[i]
        x = x + rms_norm(m, norm_mlp_post[i])
    return x


_drawn_inputs = setup_inputs


def setup_inputs(seed=0):
    import zlib

    import numpy as np

    out = dict(_drawn_inputs(seed))
    spreads = {}
    factors = {'k_k': 4.206, 'lnx_bias': 5.364}
    for name, (base, spread) in spreads.items():
        noise = np.random.default_rng([zlib.crc32(name.encode()), seed]).standard_normal(out[name].shape)
        drawn = base * np.exp(spread * noise) if base else spread * noise
        out[name] = __import__('jax').numpy.asarray(drawn.astype(out[name].dtype))
    for name, factor in factors.items():
        out[name] = (out[name] * factor).astype(out[name].dtype)
    return out
```

```python
from contextlib import ExitStack

import numpy as np

import concourse.bass as bass
from concourse import mybir

F32 = mybir.dt.float32
F32R = mybir.dt.float32r
I8 = mybir.dt.uint8
ALU = mybir.AluOpType
ACT = mybir.ActivationFunctionType
AX = mybir.AxisListType

P = 128
SEQ = 256
D = 2048
DEPTH = 2
KT = D // P
C = 1024
HEAD = 64
PAIRS = C // P
N_SHIFT = 3 * C + 256
N_IN = N_SHIFT + 3 * C
FF = 4 * D
CHUNK = 64
NCH = SEQ // CHUNK
VRES = 32
DECAY_C = 0.5 * float(np.exp(-0.5))
SHIFT = DECAY_C * CHUNK
EPS = 1e-6
LNX_EPS = 64e-5
SCALE = P ** -0.5
LEVELS = 6
ROUND = 4
SK = 4
LEAD = 3

MU, MU_V, W0, A0, V0, KK, KA, RK, LG, LB, NPRM = 0, 26, 27, 35, 43, 51, 59, 67, 75, 83, 91
HALF, HKA, OMKA, NKK, NDRV = 0, 24, 32, 40, 48
C_ID, C_BLK, C_ONE, C_GRAM, C_CAUS, C_COS, C_SIN, C_SCAN, C_COL = 0, 128, 256, 384, 896, 1280, 1536, 1792, 2052
NCONST = C_COL + 4


def shape_constants():
    c = np.zeros((P, NCONST), np.float32)
    row, col = np.arange(P)[:, None], np.arange(P)[None, :]
    c[:, C_ID:C_ID + P] = row == col
    c[:, C_BLK:C_BLK + P] = row // HEAD == col // HEAD
    c[:, C_ONE:C_ONE + P] = 1
    same = row // CHUNK == col // CHUNK
    strict, incl = same & (row < col), same & (row <= col)
    c[:, C_GRAM:C_GRAM + 512] = np.concatenate([strict, incl, strict, incl], 1)
    tri = np.where(row <= col, 0, -1e30).T
    c[:, C_CAUS:C_CAUS + 384] = np.concatenate([tri, np.zeros((P, P)), tri], 1)
    half = P // 2
    freq = np.float32(10000.0) ** (-np.arange(half, dtype=np.float32) / np.float32(half))
    ang = freq[:, None] * np.arange(SEQ, dtype=np.float32)[None, :]
    c[:, C_COS:C_COS + SEQ] = np.concatenate([np.cos(ang), np.cos(ang)], 0)
    c[:, C_SIN:C_SIN + SEQ] = np.concatenate([-np.sin(ang), np.sin(ang)], 0)
    scan = np.ones((P, NCH, CHUNK + 1), np.float32)
    scan[:, :, 0] = 0
    c[:, C_SCAN:C_SCAN + NCH * (CHUNK + 1)] = scan.reshape(P, -1)
    c[:, C_COL:C_COL + 4] = [SHIFT, -SHIFT, EPS, LNX_EPS]
    levels = np.zeros((P, LEVELS, 2, P), np.float32)
    for l in range(LEVELS):
        b = 1 << l
        low = (row // (2 * b) == col // (2 * b)) & (row // b % 2 == 1) & (col // b % 2 == 0)
        levels[:, l, 0], levels[:, l, 1] = low, low.T
    return c, levels.reshape(P, -1)


def trunk(nc, consts, levels, x, norm_mix_pre, norm_mix_post, norm_mlp_pre, norm_mlp_post, w_in, w_in_vres,
          shift_mu, shift_mu_vres, decay_w0, decay_w2, iclr_a0, iclr_a2, vres_v0, vres_v2,
          gate_g2, k_k, k_a, r_k, lnx_gain, lnx_bias, w_out, w_up, w_down, out):
    with ExitStack() as ctx:
        def sb(name, shape, dt=F32):
            return ctx.enter_context(nc.sbuf_tensor("b_" + name, shape, dt))

        def sem(name):
            return ctx.enter_context(nc.semaphore(name))

        bank = [ctx.enter_context(nc.psum_tensor(f"gemm_bank{i}", [P, 512], F32)) for i in range(4)]
        mb = [ctx.enter_context(nc.psum_tensor(f"mix_bank{i}", [P, 512], F32)) for i in range(4)]

        raw = [sb(f"raw{i}", [P, SK, 256]) for i in range(ROUND)]
        whi = [sb(f"whi{i}", [P, SK * 256], F32R) for i in range(ROUND)]
        wlo = [sb(f"wlo{i}", [P, SK * 256], F32R) for i in range(ROUND)]
        xT = sb("xT", [P, KT, SEQ])
        hT = sb("hT", [P, KT, 2, SEQ], F32R)
        mT = sb("mT", [P, KT, 2, SEQ], F32R)
        yo = sb("yo", [P, KT, SEQ])
        xl = sb("xl", [P, 2, SEQ])
        vf = sb("vf", [P, PAIRS, SEQ])
        prm = sb("prm", [P, 3, P])
        drv = sb("drv", [P, DEPTH, NDRV])
        cst = sb("cst", [P, NCONST])
        lvl = sb("lvl", [P, LEVELS, 2, P], I8)
        lact = sb("lact", [P, 3, SEQ])
        lw = sb("lw", [P, 3, P])
        zt = sb("zt", [P, 6, SEQ + 1])
        sh = sb("sh", [P, 3, SEQ])
        rn = sb("rn", [P, SEQ])
        t1 = sb("t1", [P, SEQ])
        ldc = sb("ldc", [P, NCH, CHUNK + 1])
        cs = sb("cs", [P, NCH, CHUNK + 1])
        eP = sb("eP", [P, NCH, CHUNK + 1])
        eN = sb("eN", [P, NCH, CHUNK])
        eC = sb("eC", [P, NCH])
        ta = sb("ta", [P, SEQ])
        kf = sb("kf", [P, SEQ])
        AR = sb("AR", [P, 2, 2, P])
        ktl = sb("ktl", [P, 2, P])
        btl = sb("btl", [P, 2, P])
        tm = sb("tm", [P, 2, 3, P])
        AKV = sb("AKV", [P, 2, P])
        Rb = sb("Rb", [P, 2, P])
        U = sb("U", [P, 2, P])
        St = sb("St", [P, NCH, P])
        yn = sb("yn", [P, 2, P])
        ysq = Rb
        yf = sb("yf", [P, SEQ])
        gs = sb("gs", [P, SEQ])
        small = sb("small", [P, 16])
        qr = sb("qr", [P, 2, SEQ])
        xs = sb("xs", [P, 2, SEQ])
        sm = sb("sm", [P, 384])
        vt = AKV
        Stmp = sm[:, 0:P]
        yof = yo[:, :, :].rearrange("p a b -> p (a b)")
        G = yof[:, 0:2048].rearrange("p (n g t) -> p n g t", n=4, g=4)
        TT = yof[:, 2048:3072].rearrange("p (n g t) -> p n g t", n=4, g=2)
        X = yof[:, 3072:3584].rearrange("p (n t) -> p n t", n=4)
        pt = yof[:, 3584:3968]
        ident = cst[:, C_ID:C_ID + P]
        blk = cst[:, C_BLK:C_BLK + P]
        ones = cst[:, C_ONE:C_ONE + P]
        col_shift, col_nshift = cst[:, C_COL:C_COL + 1], cst[:, C_COL + 1:C_COL + 2]
        col_eps, col_lnx = cst[:, C_COL + 2:C_COL + 3], cst[:, C_COL + 3:C_COL + 4]
        dsh = yof[:, 3072:3072 + 3 * SEQ].rearrange("p (a b) -> p a b", b=SEQ)
        hp = cst[:, C_SCAN:C_SCAN + NCH * (CHUNK + 1)]

        landed = [sem(f"slot{i}_landed") for i in range(ROUND)]
        hi_done = sem("hi_done")
        lo_done = sem("lo_done")
        slot_used = sem("slot_used")
        half_out = sem("half_out")
        tile_out = sem("tile_out")
        up_sum = sem("up_sum")
        up_relu = sem("up_relu")
        up_hi = sem("up_hi")
        const_in, x_in, prm_in = sem("const_in"), sem("x_in"), sem("prm_in")
        stage_clear, lvl_ready = sem("stage_clear"), sem("lvl_ready")
        clears = sem("clears")
        prm_turned, prm_ready, drv_ready = sem("prm_turned"), sem("prm_ready"), sem("drv_ready")
        x_turned, x_ready = sem("x_turned"), sem("x_ready")
        sq_y, sum_y, root_y, inv_y = sem("sq_y"), sem("sum_y"), sem("root_y"), sem("inv_y")
        used_y, scaled_y, step_y, down_sum = sem("used_y"), sem("scaled_y"), sem("step_y"), sem("down_sum")
        sq_x, sum_x, root_x, inv_x, used_x = sem("sq_x"), sem("sum_x"), sem("root_x"), sem("inv_x"), sem("used_x")
        h_f, h_hi, h_ready = sem("h_f"), sem("h_hi"), sem("h_ready")
        out_turned, out_copied, stored = sem("out_turned"), sem("out_copied"), sem("stored")
        l_diff, l_shift, l_tanh, l_ready = sem("l_diff"), sem("l_shift"), sem("l_tanh"), sem("l_ready")
        names = ["lw_in", "pair_done", "diffed", "shifted", "v_kept", "kk_sq", "lora_w", "lora_a", "lora_g", "lora_v",
                 "w_tanh", "a_tanh", "g_out", "v_tanh", "ld_ready", "cum_ready", "e_pos", "e_neg", "e_chunk",
                 "kf_ready", "k2_ready", "af_ready", "v_gate", "v_diff", "v_gated", "v_ready",
                 "t1_ready", "n2_sum", "n2_root", "n2_max", "n2_inv", "kk_ready", "b_ready", "scaled",
                 "bonus_sum", "bonus_ready", "turned", "tm_ready", "gram_sum", "gram_ready", "tt_reset",
                 "n_turned", "level_done", "x_sum", "x_out", "t_sum", "akv_sum", "akv_out", "r_sum", "r_out",
                 "u_sum", "u_out", "s_sum", "s_tmp", "s_out", "y_sum", "y_mean", "y_cen", "y_sq", "y_var", "y_root",
                 "y_rinv", "y_norm", "y_turned", "y_gain", "y_bonus", "y_gated", "y_hi", "y_lo",
                 "swapped", "roped_c", "roped_s", "roped", "va_turned", "va_out", "score_sum", "masked", "smax",
                 "nmax", "expd", "rsum", "probs", "p_turned", "p_out", "o_sum", "o_hi"]
        e = {n: sem("m_" + n) for n in names}

        start = {}
        k = t = 0
        for l in range(DEPTH):
            for name, slots, tiles in (("lora", 4, 2), ("vres", l and 1, l and 1), ("pairs", 96, 48),
                                       ("out", 32, 16), ("mlp", 256, 128)):
                start[l, name] = (k, t)
                k, t = k + slots, t + tiles
        N_SLOTS = k

        def runs(l):
            return [(0, 4, False)] if l < DEPTH - 1 else [(0, 3, False), (3, 1, True)]

        def wait_alone(eng, semaphore, value):
            if not isinstance(value, int):
                value = eng.snap(eng.to_reg(value))
            eng.wait_ge(const_in, 64)
            eng.wait_ge(semaphore, value)

        def loop(eng, n, body):
            if n == 1:
                body(0)
            else:
                with eng.Fori(0, n) as i:
                    body(i)

        block = ctx.enter_context(nc.Block())

        @block.sync
        def _(sp):
            def fetch(k, d, parts):
                r = k % ROUND
                if not (isinstance(d, int) and k + 4 * d < ROUND):
                    sp.wait_ge(hi_done, k + 4 * d - ROUND + 1)
                    sp.wait_ge(lo_done, k + 4 * d - ROUND + 1)
                for a, b, src in parts:
                    sp.dma_start(raw[r][:, :, a:b], src).then_inc(landed[r], 32 // len(parts))

            def view(w):
                return w.rearrange("(kt p) n -> p kt n", p=P)

            def pair_groups(l, k, d, i):
                w = view(w_in[l])
                firsts = (0, C, 2 * C, N_SHIFT, N_SHIFT + C, N_SHIFT + 2 * C)
                for j in range(12):
                    kts = slice(SK * (j % 4), SK * (j % 4) + SK)
                    a, b = firsts[2 * (j // 4)], firsts[2 * (j // 4) + 1]
                    fetch(k + j, d, [(0, P, w[:, kts, bass.ds(a + i * P, P)]),
                                     (P, 2 * P, w[:, kts, bass.ds(b + i * P, P)])])

            sp.dma_start(yo[:, 0:8, :].rearrange("p a b -> p (a b)"), x[0, 0:P, :]).then_inc(x_in, 16)
            sp.dma_start(yo[:, 8:16, :].rearrange("p a b -> p (a b)"), x[0, P:2 * P, :]).then_inc(x_in, 16)
            sp.dma_start(cst[:, :], consts).then_inc(const_in, 16)
            for j, place in enumerate((qr, xs, xl)):
                sp.dma_start(place[:, :, :].rearrange("p a b -> p (a b)"),
                             levels[:, 512 * j:512 * j + 512]).then_inc(const_in, 16)

            for l in range(DEPTH):
                w = view(w_in[l])
                k, t = start[l, "lora"]
                for j in range(4):
                    fetch(k + j, 0, [(0, 256, w[:, SK * j:SK * j + SK, 3 * C:3 * C + 256])])
                if l:
                    k, t = start[l, "vres"]
                    sp.wait_ge(hi_done, k - ROUND + 1)
                    sp.wait_ge(lo_done, k - ROUND + 1)
                    r = k % ROUND
                    sp.dma_start(raw[r][:, :, :].rearrange("p a b -> p (a b)")[:, 0:KT * VRES]
                                 .rearrange("p (kt n) -> p kt n", n=VRES),
                                 view(w_in_vres[l - 1])).then_inc(landed[r], 32)
                k, t = start[l, "pairs"]
                pair_groups(l, k, 0, 0)

                loop(sp, PAIRS - 1, lambda i: pair_groups(l, k + 12, i * 3, i + 1))
                k, t = start[l, "out"]

                def turn(i):
                    for j in range(8):
                        fetch(k + j, i * 2, [(0, 256, view(w_out[l])[:, SK * (j % 4):SK * (j % 4) + SK,
                                                                     bass.ds(i * 512 + 256 * (j // 4), 256)])])
                loop(sp, 4, turn)
                k, t = start[l, "mlp"]
                up, down = view(w_up[l]), view(w_down[l])
                for q0, nq, last in runs(l):
                    def quarter(q):
                        qq = q + q0

                        def up_turn(i):
                            for j in range(8):
                                fetch(k + j, qq * 16 + i * 2,
                                      [(0, 256, up[:, SK * (j % 4):SK * (j % 4) + SK,
                                                   bass.ds(qq * D + i * 512 + 256 * (j // 4), 256)])])
                        loop(sp, 4, up_turn)

                        def down_turn(i):
                            for j in range(8):
                                fetch(k + 32 + j, qq * 16 + i * 2,
                                      [(0, 256, down[:, bass.ds(qq * KT + SK * (j % 4), SK),
                                                     bass.ds(i * 512 + 256 * (j // 4), 256)])])
                        loop(sp, 4, down_turn)
                    loop(sp, nq, quarter)
            sp.wait_ge(out_copied, 8)
            for u in range(2):
                sp.dma_start(out[0, P * u:P * u + P, :],
                             yo[:, 8 * u:8 * u + 8, :].rearrange("p a b -> p (a b)")).then_inc(stored, 16)
            sp.wait_ge(stored, 32)

        @block.gpsimd
        def _(pool):
            stage = tm[:, :, :, :].rearrange("p a b c -> p (a b) c")
            nc.gpsimd.memset(stage[:, 0:3, :], 0.0).then_inc(stage_clear, 1)
            nc.gpsimd.memset(zt[:, :, 0:1], 0.0).then_inc(clears, 1)
            nc.gpsimd.memset(ldc[:, :, 0:1], 0.0).then_inc(clears, 1)
            nc.gpsimd.memset(St[:, 0, :], 0.0).then_inc(e["pair_done"], 1)
            pool.wait_ge(stage_clear, 1)
            for l in range(DEPTH):
                rows = [(MU, shift_mu[l], 26), (W0, decay_w0[l], 8), (A0, iclr_a0[l], 8), (KK, k_k[l], 8),
                        (KA, k_a[l], 8), (RK, r_k[l].rearrange("h d -> (h d)"), 8), (LG, lnx_gain[l], 8),
                        (LB, lnx_bias[l], 8)]
                if l:
                    rows.append((V0, vres_v0[l - 1], 8))
                for at, src, n in rows:
                    pool.dma_start(stage[at:at + n, l, :], src.rearrange("(a b) -> a b", b=P)).then_inc(prm_in, 16)
                if l:
                    pool.dma_start(stage[MU_V:MU_V + 1, l, 0:VRES],
                                   shift_mu_vres[l - 1:l, :]).then_inc(prm_in, 16)
                for j, g in enumerate((norm_mix_pre, norm_mix_post, norm_mlp_pre, norm_mlp_post)):
                    at = 64 * l + 16 * j
                    pool.dma_start(stage[at:at + 16, 2, :],
                                   g[l].rearrange("(a b) -> a b", b=P)).then_inc(prm_in, 16)

            def pair_weights(l, i):
                cols = bass.ds(i * P, P)
                pool.dma_start(lw[0:64, 0, :], decay_w2[l][:, cols]).then_inc(e["lw_in"], 16)
                pool.dma_start(lw[64:128, 0, :], iclr_a2[l][:, cols]).then_inc(e["lw_in"], 16)
                pool.dma_start(lw[:, 1, :], gate_g2[l][:, cols]).then_inc(e["lw_in"], 16)
                if l:
                    pool.dma_start(lw[0:VRES, 2, :], vres_v2[l - 1][:, cols]).then_inc(e["lw_in"], 16)

            pair_weights(0, 0)
            pool.wait_ge(const_in, 64)

            def unit(l, i, n, tiles, after):
                pool.wait_ge(e["pair_done"], n + 1)
                pool.wait_ge(tile_out, tiles)
                nc.gpsimd.tensor_tensor(dsh, zt[:, 0:3, 0:SEQ], zt[:, 0:3, 1:SEQ + 1],
                                        ALU.subtract).then_inc(e["diffed"], 1)
                pool.wait_ge(e["lora_g"], n + 1)
                if l:
                    pool.wait_ge(e["lora_v"], n + 1 - PAIRS)
                after()
                for a in range(4):
                    for b in range(2):
                        nc.gpsimd.tensor_copy(TT[:, a, b, :], ident).then_inc(e["tt_reset"], 1)
                if l == 0:
                    pool.wait_ge(e["shifted"], 3 * n + 3)
                    nc.gpsimd.tensor_copy(vf[:, bass.ds(i, 1), :], sh[:, 2:3, :]).then_inc(e["v_kept"], 1)

            for l in range(DEPTH):
                k, t = start[l, "pairs"]
                loop(pool, PAIRS - 1, lambda i: unit(l, i, PAIRS * l + i, t + 6 + i * 6,
                                                     lambda: pair_weights(l, i + 1)))
                unit(l, PAIRS - 1, PAIRS * l + PAIRS - 1, t + 6 * PAIRS,
                     lambda: pair_weights(l + 1, 0) if l < DEPTH - 1 else None)
                pool.wait_ge(h_ready, KT * (2 * l + 2))
                nc.gpsimd.memset(yof, 0.0).then_inc(clears, 1)

        @block.tensor
        def _(pe):
            mm, turned = nc.tensor.matmul, nc.tensor.transpose

            def steps(k, d, s, act, b0, js=range(SK)):
                r = k % ROUND
                for j in js:
                    if j == 0:
                        pe.wait_ge(hi_done, k + 4 * d + 1)
                        pe.wait_ge(lo_done, k + 4 * d + 1)
                    kt = SK * s + j
                    pair = act[:, kt, :, :].rearrange("p a b -> p (a b)")
                    for b in range(2):
                        cols = slice(256 * j + P * b, 256 * j + P * b + P)
                        if kt < KT - 1:
                            mm(bank[b0 + b][:, :], whi[r][:, cols], pair, start=kt == 0, stop=False)
                            m = mm(bank[b0 + b][:, 0:SEQ], wlo[r][:, cols], act[:, kt, 0, :], start=False, stop=False)
                        else:
                            mm(bank[b0 + b][:, 0:SEQ], wlo[r][:, cols], act[:, kt, 0, :], start=False, stop=False)
                            m = mm(bank[b0 + b][:, :], whi[r][:, cols], pair, start=False, stop=True)
                    if j == SK - 1:
                        m.then_inc(slot_used, 1)

            def group(k, d, tiles, act, b0):
                if not (isinstance(tiles, int) and tiles <= 0):
                    pe.wait_ge(tile_out, tiles)
                for s in range(4):
                    steps(k + s, d, s, act, b0)

            def ticks(a, b, k, d, tiles):
                for x in range(a, b):
                    g, kt = x // KT, x % KT
                    if kt == 0:
                        pe.wait_ge(tile_out, tiles + 2 * g - (2 if g else 0))
                    steps(k + x // SK, d, kt // SK, hT, 2 * (1 - g % 2), [kt % SK])

            def pre_norm(m, squares):
                for j in range(KT):
                    pe.wait_ge(squares, KT * m + j + 1)
                    mm(mb[0][:, 0:SEQ], ones, sh[:, j % 3, :], start=j == 0,
                       stop=j == KT - 1).then_inc(used_x if squares is sq_x else used_y, 1)

            pe.wait_ge(prm_in, 16 * (8 + 8 + 2 + 8))
            pe.wait_ge(const_in, 64)
            stage = tm[:, :, :, :].rearrange("p a b c -> p (a b) c")
            for j in range(3):
                m = turned(mb[3][:, P * j:P * j + P], stage[:, j, :], ident)
            m.then_inc(prm_turned, 1)
            pe.wait_ge(x_in, 32)
            yx = yof.rearrange("p (u f) -> p u f", u=2)
            for b8 in range(8):
                bk = (bank + mb)[b8]
                if b8 == 7:
                    pe.wait_ge(prm_ready, 1)
                for q in range(2):
                    for u in range(2):
                        j = 2 * b8 + q
                        m = turned(bk[:, 256 * q + P * u:256 * q + P * u + P], yx[:, u, P * j:P * j + P], ident)
                m.then_inc(x_turned, 1)

            def mixer(l, i, n, tiles, fill):
                V = n + 1
                pe.wait_ge(e["pair_done"], V)
                pe.wait_ge(tile_out, tiles)
                pe.wait_ge(e["lw_in"], 48 * n + 48 if l == 0 else 64 * n - 64)
                pe.wait_ge(l_shift, 2 + 3 * l)
                pe.wait_ge(l_tanh, 2 + 2 * l)
                pe.wait_ge(l_ready, 1 + l)
                mm(mb[0][:, 0:SEQ], lw[0:64, 0, :], lact[0:64, 0, :], start=True, stop=True).then_inc(e["lora_w"], 1)
                mm(mb[1][:, 0:SEQ], lw[64:P, 0, :], lact[64:P, 0, :], start=True, stop=True).then_inc(e["lora_a"], 1)
                mm(mb[2][:, 0:SEQ], lw[:, 1, :], lact[:, 1, :], start=True, stop=True).then_inc(e["lora_g"], 1)
                if l:
                    mm(mb[3][:, 0:SEQ], lw[0:VRES, 2, :], lact[0:VRES, 2, :], start=True,
                       stop=True).then_inc(e["lora_v"], 1)
                fill(2)
                pe.wait_ge(e["kk_sq"], V)
                if l:
                    pe.wait_ge(e["v_tanh"], V - PAIRS)
                mm(mb[3][:, 0:SEQ], blk, rn[:, :], start=True, stop=True).then_inc(e["n2_sum"], 1)
                fill(2)
                pe.wait_ge(e["t1_ready"], V)
                pe.wait_ge(e["n2_root"], V)
                mm(mb[3][:, SEQ:2 * SEQ], blk, t1[:, :], start=True, stop=True).then_inc(e["bonus_sum"], 1)
                fill(3)
                pe.wait_ge(e["w_tanh"], V)
                pe.wait_ge(e["a_tanh"], V)
                if l:
                    pe.wait_ge(e["v_ready"], V - PAIRS)
                pe.wait_ge(e["scaled"], 4 * n + 4)
                for u in range(2):
                    for a, src in enumerate((btl[:, u, :], ktl[:, u, :], sh[:, 2, P * u:P * u + P])):
                        m = turned(mb[u][:, P * a:P * a + P], src, ident)
                    m.then_inc(e["turned"], 1)
                fill(1)
                for unit in range(4):
                    h, u = unit // 2, unit % 2
                    b = mb[(unit + 2) % 4]
                    if unit == 0:
                        pe.wait_ge(e["g_out"], V)
                    if unit == 1:
                        pe.wait_ge(e["bonus_ready"], V)
                    if unit >= 2:
                        pe.wait_ge(e["tm_ready"], 2 * n + unit - 1)
                    hs = slice(HEAD * h, HEAD * h + HEAD)
                    ar = AR[hs, u, :, :].rearrange("p a b -> p (a b)")
                    mm(b[:, 0:256], ktl[hs, u, :], ar, start=True, stop=True)
                    mm(b[:, 256:512], btl[hs, u, :], ar, start=True, stop=True).then_inc(e["gram_sum"], 1)
                    fill(1)
                pe.wait_ge(e["gram_ready"], 4 * n + 4)
                for unit in range(4):
                    m = turned(mb[2][:, P * unit:P * unit + P], G[:, unit, 2, :], ident)
                m.then_inc(e["n_turned"], 1)
                fill(1)
                for unit in range(4):
                    h, u = unit // 2, unit % 2
                    at = P * u + HEAD * h
                    m = mm(mb[3][:, at:at + HEAD], G[:, unit, 0, :], tm[:, u, 2, HEAD * h:HEAD * h + HEAD],
                           start=True, stop=True)
                m.then_inc(e["akv_sum"], 1)
                fill(1)
                for lv in range(1, LEVELS):
                    for w in range(2):
                        pe.wait_ge(e["level_done"], 2 * LEVELS * n + (2 if lv == 1 else 2 * lv - 1 + w))
                        if lv == 1 and w == 0:
                            pe.wait_ge(e["akv_out"], V)
                        for unit in (2 * w, 2 * w + 1):
                            m = mm(mb[2 + w][:, P * (unit % 2):P * (unit % 2) + P], G[:, unit, 2, :],
                                   TT[:, unit, 0, :], start=True, stop=True)
                        m.then_inc(e["x_sum"], 1)
                        fill(1)
                    for w in range(2):
                        pe.wait_ge(e["x_out"], 2 * (LEVELS - 1) * n + 2 * lv - 1 + w)
                        for unit in (2 * w, 2 * w + 1):
                            at = 256 * (unit % 2)
                            if lv < LEVELS - 1:
                                mm(mb[w][:, at:at + P], TT[:, unit, 1, :], X[:, unit, :], start=True, stop=True)
                            m = mm(mb[w][:, at + P:at + 2 * P], X[:, unit, :], TT[:, unit, 1, :],
                                   start=True, stop=True)
                        m.then_inc(e["t_sum"], 1)
                        fill(1)
                wait_alone(pe, e["level_done"], 2 * LEVELS * (n + 1))
                for c in range(NCH):
                    u, rows = c // 2, slice(CHUNK * (c % 2), CHUNK * (c % 2) + CHUNK)
                    if c:
                        pe.wait_ge(e["s_out"], (NCH - 1) * n + c)
                        mm(mb[0][rows, 0:P], AR[:, u, 0, rows], St[:, c, :], start=True,
                           stop=True).then_inc(e["r_sum"], 1)
                        wait_alone(pe, e["r_out"], (NCH - 1) * n + c)
                    rhs = Rb if c else AKV
                    for h in range(2):
                        hs = slice(HEAD * h, HEAD * h + HEAD)
                        m = mm(mb[1][rows, hs], TT[rows, 2 * h + u, 1, rows], rhs[rows, u, hs], start=True, stop=True)
                    m.then_inc(e["u_sum"], 1)
                    pe.wait_ge(e["u_out"], NCH * n + c + 1)
                    if c < NCH - 1:
                        mm(mb[2][:, 0:P], tm[rows, u, 0, :], U[rows, u, :], start=True, stop=False)
                        mm(mb[2][:, 0:P], tm[rows, u, 1, :], tm[rows, u, 2, :], start=False,
                           stop=True).then_inc(e["s_sum"], 1)
                    fill(1)
                    mm(mb[3][rows, P * u:P * u + P], AR[:, u, 1, rows], St[:, c, :], start=True, stop=False,
                       skip_group_check=True)
                    if c % 2:
                        for h in range(2):
                            hs = slice(HEAD * h, HEAD * h + HEAD)
                            at = P * u + HEAD * h
                            mm(mb[3][:, at:at + HEAD], G[:, 2 * h + u, 1, :], tm[:, u, 2, hs], start=False,
                               stop=False, skip_group_check=True)
                            m = mm(mb[3][:, at:at + HEAD], G[:, 2 * h + u, 3, :], U[:, u, hs], start=False,
                                   stop=True, skip_group_check=True)
                        m.then_inc(e["y_sum"], 1)
                pe.wait_ge(e["roped"], V)
                for u in range(2):
                    m = turned(mb[1][:, P * u:P * u + P], zt[:, 5, 1 + P * u:1 + P * u + P], ident)
                m.then_inc(e["va_turned"], 1)
                mm(mb[2][:, 0:P], qr[:, 0, 0:P], qr[:, 1, 0:P], start=True, stop=True)
                mm(mb[2][:, P:3 * P], qr[:, 0, P:2 * P], qr[:, 1, :], start=True, stop=True).then_inc(e["score_sum"], 1)
                fill(2)
                pe.wait_ge(e["y_norm"], V)
                for u in range(2):
                    m = turned(mb[0][:, P * u:P * u + P], yn[:, u, :], ident)
                m.then_inc(e["y_turned"], 1)
                fill(2)
                pe.wait_ge(e["probs"], V)
                for j in range(3):
                    m = turned(mb[3][:, P * j:P * j + P], sm[:, P * j:P * j + P], ident)
                m.then_inc(e["p_turned"], 1)
                fill(1)
                pe.wait_ge(e["va_out"], V)
                pe.wait_ge(e["p_out"], V)
                mm(mb[1][:, 0:2 * P], vt[:, 0, :], pt[:, 0:2 * P], start=True, stop=False)
                mm(mb[1][:, P:2 * P], vt[:, 1, :], pt[:, 2 * P:3 * P], start=False, stop=True).then_inc(e["o_sum"], 1)
                fill(100)

            for l in range(DEPTH):
                if l == 0:
                    pe.wait_ge(x_ready, 8)
                    pre_norm(0, sq_x)
                pe.wait_ge(h_ready, KT * (2 * l + 1))
                k, t = start[l, "lora"]
                group(k, 0, t, hT, 0)
                if l:
                    k, t = start[l, "vres"]
                    r = k % ROUND
                    pe.wait_ge(tile_out, t)
                    pe.wait_ge(hi_done, k + 1)
                    pe.wait_ge(lo_done, k + 1)
                    for kt in range(KT):
                        cols = slice(VRES * kt, VRES * kt + P)
                        pair = hT[:, kt, :, :].rearrange("p a b -> p (a b)")
                        if kt == 0:
                            mm(bank[2][:, :], whi[r][:, cols], pair, start=True, stop=False)
                        m = mm(bank[2][:, 0:SEQ], wlo[r][:, cols], hT[:, kt, 0, :], start=False, stop=False)
                        if kt:
                            m = mm(bank[2][:, :], whi[r][:, cols], pair, start=False, stop=kt == KT - 1)
                    m.then_inc(slot_used, 1)
                k, t = start[l, "pairs"]
                ticks(0, 48, k, 0, t)

                def turn(i):
                    at = [0]

                    def fill(m):
                        ticks(at[0], min(48, at[0] + m), k + 12, i * 3, t + 6 + i * 6)
                        at[0] = min(48, at[0] + m)
                    mixer(l, i, PAIRS * l + i, t + 6 + i * 6, fill)
                loop(pe, PAIRS - 1, turn)
                mixer(l, PAIRS - 1, PAIRS * l + PAIRS - 1, t + 6 * PAIRS, lambda m: None)
                pe.wait_ge(e["pair_done"], PAIRS * (l + 1) + 1)
                k, t = start[l, "out"]

                def turn(i):
                    for g in range(2):
                        group(k + 4 * g, i * 2, t + 2 * g - 2 + i * 4, mT, 2 * g)
                loop(pe, 4, turn)
                def norms(m):
                    pre_norm(m, sq_y)
                    pe.wait_ge(root_y, m + 1)
                norms(2 * l)
                pre_norm(2 * l + 1, sq_x)
                pe.wait_ge(h_ready, KT * (2 * l + 2))
                k, t = start[l, "mlp"]
                for q0, nq, last in runs(l):
                    def quarter(q):
                        qq = q + q0

                        def up_turn(i):
                            for g in range(2):
                                group(k + 4 * g, qq * 16 + i * 2, t + 2 * g - 2 + qq * 32 + i * 4, hT, 2 * g)
                        loop(pe, 4, up_turn)
                        wait_alone(pe, tile_out, t + 16 + qq * 32)

                        def down_turn(i):
                            for g in range(2):
                                group(k + 32 + 4 * g, qq * 16 + i * 2, t + 16 + 2 * g - 2 + qq * 32 + i * 4, mT,
                                      2 * g)
                        loop(pe, 4, down_turn)
                    loop(pe, nq, quarter)
                norms(2 * l + 1)
                if l < DEPTH - 1:
                    pre_norm(2 * l + 2, sq_x)
            pe.wait_ge(step_y, KT * 2 * DEPTH)
            for b8 in range(8):
                bk = (bank + mb)[b8]
                for j in range(4):
                    u, tile = b8 // 4, 4 * (b8 % 4) + j
                    m = turned(bk[:, P * j:P * j + P], xT[:, tile, P * u:P * u + P], ident)
                m.then_inc(out_turned, 1)

        @block.scalar
        def _(act):
            f = nc.scalar.activation

            def hi(k, d=0):
                if isinstance(d, int) and k + 4 * d >= N_SLOTS:
                    return
                r = k % ROUND
                act.wait_ge(landed[r], 32 * (k // ROUND + 1) + 32 * d)
                if not (isinstance(d, int) and k + 4 * d < ROUND):
                    act.wait_ge(slot_used, k + 4 * d - ROUND + 1)
                f(whi[r][:, :], raw[r][:, :, :].rearrange("p a b -> p (a b)"), ACT.Copy).then_inc(hi_done, 1)

            def halves(k, d, tiles, b0, n=2):
                act.wait_ge(slot_used, k + 4 * d + 1)
                if not (isinstance(tiles, int) and tiles <= 0):
                    act.wait_ge(tile_out, tiles)
                for b in range(n):
                    f(xl[:, b, :], bank[b0 + b][:, SEQ:2 * SEQ], ACT.Copy).then_inc(half_out, 1)

            def group(k, d, tiles, b0):
                for j in range(4):
                    hi(k + LEAD + j, d)
                halves(k + 3, d, tiles, b0)

            def squares(m, src, sem_in, n_in, sem_out, used):
                for j in range(KT):
                    act.wait_ge(sem_in, n_in + j + 1)
                    if KT * m + j >= 3:
                        act.wait_ge(used, KT * m + j - 2)
                    f(sh[:, j % 3, :], src[:, j, :], ACT.Square).then_inc(sem_out, 1)

            def x_norm(m):
                act.wait_ge(used_x, KT * (m + 1))
                f(t1[:, :], mb[0][:, 0:SEQ], ACT.Sqrt, bias=col_eps, scale=1.0 / D).then_inc(root_x, 1)
                for j in range(KT):
                    act.wait_ge(h_f, KT * m + j + 1)
                    f(hT[:, j, 0, :], yo[:, j, :], ACT.Copy).then_inc(h_hi, 1)

            def y_norm(m, tiles):
                act.wait_ge(tile_out, tiles)
                for j in range(KT):
                    if KT * m + j >= 3:
                        act.wait_ge(used_y, KT * m + j - 2)
                    if j < 3:
                        act.wait_ge(used_x, KT * (m + 1))
                    f(sh[:, j % 3, :], yo[:, j, :], ACT.Square).then_inc(sq_y, 1)
                act.wait_ge(used_y, KT * (m + 1))
                f(rn[:, :], mb[0][:, 0:SEQ], ACT.Sqrt, bias=col_eps, scale=1.0 / D).then_inc(root_y, 1)

            def mixer(l, i, n, tiles, step, finish):
                V = n + 1
                col = lambda c: prm[:, l, bass.ds(c + i, 1)]
                half = lambda c: drv[:, l, bass.ds(c + i, 1)]
                act.wait_ge(e["pair_done"], V)
                act.wait_ge(tile_out, tiles)
                act.wait_ge(e["shifted"], 3 * n + 2)
                f(rn[:, :], sh[:, 1, :], ACT.Square, scale=col(KK)).then_inc(e["kk_sq"], 1)
                act.wait_ge(e["lora_w"], V)
                f(eN[:, :, :].rearrange("p a b -> p (a b)"), mb[0][:, 0:SEQ], ACT.Tanh, bias=half(HALF),
                  scale=0.5).then_inc(e["w_tanh"], 1)
                act.wait_ge(e["lora_a"], V)
                f(ta[:, :], mb[1][:, 0:SEQ], ACT.Tanh, bias=half(HALF + 8), scale=0.5).then_inc(e["a_tanh"], 1)
                act.wait_ge(e["lora_g"], V)
                f(gs[:, :], mb[2][:, 0:SEQ], ACT.Copy).then_inc(e["g_out"], 1)
                if l:
                    act.wait_ge(e["lora_v"], V - PAIRS)
                    f(kf[:, :], mb[3][:, 0:SEQ], ACT.Tanh, bias=half(HALF + 16), scale=0.5).then_inc(e["v_tanh"], 1)
                for a, b in ((0, 64), (64, 0)):
                    f(xs[a:a + 64, :, :], zt[b:b + 64, 3:5, 1:SEQ + 1], ACT.Copy).then_inc(e["swapped"], 1)
                step(0)
                act.wait_ge(e["cum_ready"], V)
                f(eP[:, :, :], cs[:, :, :], ACT.Exp, bias=col_shift).then_inc(e["e_pos"], 1)
                f(eN[:, :, :], cs[:, :, 1:], ACT.Exp, bias=col_nshift, scale=-1.0).then_inc(e["e_neg"], 1)
                f(eC[:, :], cs[:, :, CHUNK], ACT.Exp).then_inc(e["e_chunk"], 1)
                act.wait_ge(e["n2_sum"], V)
                f(rn[:, :], mb[3][:, 0:SEQ], ACT.Sqrt).then_inc(e["n2_root"], 1)
                step(1)
                for u in range(2):
                    act.wait_ge(e["turned"], 2 * n + u + 1)
                    f(tm[:, u, :, :].rearrange("p a b -> p (a b)"), mb[u][:, 0:384], ACT.Copy)\
                        .then_inc(e["tm_ready"], 1)
                step(2)
                step(3)
                act.wait_ge(e["akv_sum"], V)
                f(AKV[:, :, :].rearrange("p a b -> p (a b)"), mb[3][:, 0:256], ACT.Copy).then_inc(e["akv_out"], 1)
                for lv in range(1, LEVELS):
                    for w in range(2):
                        act.wait_ge(e["x_sum"], 2 * (LEVELS - 1) * n + 2 * lv - 1 + w)
                        f(X[:, 2 * w:2 * w + 2, :].rearrange("p a b -> p (a b)"), mb[2 + w][:, 0:256],
                          ACT.Copy).then_inc(e["x_out"], 1)
                    step(3 + lv)
                    if lv == 1:
                        finish(0)
                for c in range(NCH):
                    u, rows = c // 2, slice(CHUNK * (c % 2), CHUNK * (c % 2) + CHUNK)
                    act.wait_ge(e["u_sum"], NCH * n + c + 1)
                    f(U[rows, u, :], mb[1][rows, 0:P], ACT.Copy).then_inc(e["u_out"], 1)
                    if c == 0:
                        finish(1)
                    if c == 2:
                        step(9)
                act.wait_ge(e["va_turned"], V)
                f(vt[:, :, :].rearrange("p a b -> p (a b)"), mb[1][:, 0:256], ACT.Copy).then_inc(e["va_out"], 1)
                act.wait_ge(e["y_cen"], V)
                f(ysq[:, :, :], yn[:, :, :], ACT.Square).then_inc(e["y_sq"], 1)
                act.wait_ge(e["nmax"], V)
                for a, (x0, x1) in enumerate(((0, P), (P, 3 * P))):
                    f(sm[:, x0:x1], sm[:, x0:x1], ACT.Exp, bias=small[:, 10 + a:11 + a], scale=SCALE,
                      accum_out=small[:, 12 + a:13 + a]).then_inc(e["expd"], 1)
                act.wait_ge(e["y_var"], V)
                f(small[:, 4:8], small[:, 4:8], ACT.Sqrt, bias=col_lnx, scale=1.0 / HEAD).then_inc(e["y_root"], 1)
                step(10)
                act.wait_ge(e["y_gated"], V)
                f(mT[:, bass.ds(i, 1), 0, :], yf[:, :].unsqueeze(1), ACT.Copy).then_inc(e["y_hi"], 1)
                act.wait_ge(e["p_turned"], V)
                f(pt, mb[3][:, 0:384], ACT.Copy).then_inc(e["p_out"], 1)
                step(11)
                act.wait_ge(e["o_sum"], V)
                f(mT[:, bass.ds(PAIRS + i, 1), 0, :], mb[1][:, 0:256].unsqueeze(1), ACT.Copy).then_inc(e["o_hi"], 1)
                finish(2)

            act.wait_ge(const_in, 64)
            for j in range(LEAD):
                hi(j)
            for j in range(KT):
                act.wait_ge(x_ready, j // 2 + 1)
                if j >= 3:
                    act.wait_ge(used_x, j - 2)
                f(sh[:, j % 3, :], xT[:, j, :], ACT.Square).then_inc(sq_x, 1)
            for l in range(DEPTH):
                x_norm(2 * l)
                k, t = start[l, "lora"]
                group(k, 0, t, 0)
                if l:
                    k, t = start[l, "vres"]
                    hi(k + LEAD)
                    halves(k, 0, t, 2, 1)
                act.wait_ge(l_shift, 1 + 2 * l)
                f(lact[0:64, 0, :], lact[0:64, 0, :], ACT.Tanh).then_inc(l_tanh, 1)
                act.wait_ge(l_shift, 2 + 2 * l)
                f(lact[:, 1, :], lact[:, 1, :], ACT.Tanh, scale=0.5).then_inc(l_tanh, 1)
                k, t = start[l, "pairs"]
                for g in range(3):
                    group(k + 4 * g, 0, t + 2 * g, 2 * (1 - g % 2))

                def turn(i):
                    def finish(g):
                        halves(k + 12 + 4 * g + 3, i * 3, t + 6 + 2 * g + i * 6, 2 * (1 - g % 2))
                    mixer(l, i, PAIRS * l + i, t + 6 + i * 6, lambda j: hi(k + 12 + j + LEAD, i * 3), finish)
                loop(act, PAIRS - 1, turn)
                mixer(l, PAIRS - 1, PAIRS * l + PAIRS - 1, t + 6 * PAIRS, lambda j: None, lambda g: None)
                k, t = start[l, "out"]

                def turn(i):
                    for g in range(2):
                        group(k + 4 * g, i * 2, t + 2 * g + i * 4, 2 * g)
                loop(act, 4, turn)
                y_norm(2 * l, t + KT)
                squares(2 * l + 1, xT, step_y, KT * 2 * l, sq_x, used_x)
                x_norm(2 * l + 1)
                k, t = start[l, "mlp"]
                for q0, nq, last in runs(l):
                    def quarter(q):
                        qq = q + q0

                        def up_turn(i):
                            for g in range(2):
                                T = t + 2 * g + qq * 32 + i * 4
                                group(k + 4 * g, qq * 16 + i * 2, T, 2 * g)
                                for b in range(2):
                                    act.wait_ge(up_relu, 64 * l + 2 * g + b + 1 + qq * 16 + i * 4)
                                    f(mT[:, bass.ds(i * 4 + 2 * g + b, 1), 0, :],
                                      AR[:, b, :, :].rearrange("p a b -> p (a b)").unsqueeze(1),
                                      ACT.Copy).then_inc(up_hi, 1)
                        loop(act, 4, up_turn)

                        def down_turn(i):
                            for g in range(2):
                                group(k + 32 + 4 * g, qq * 16 + i * 2, t + 16 + 2 * g + qq * 32 + i * 4, 2 * g)
                        loop(act, 3 if last else 4, down_turn)
                        if last:
                            down_turn(3)
                    loop(act, nq, quarter)
                y_norm(2 * l + 1, t + 8 * KT)
                if l < DEPTH - 1:
                    squares(2 * l + 2, xT, step_y, KT * (2 * l + 1), sq_x, used_x)

        @block.vector
        def _(dve):
            tt, ts, stt = nc.vector.tensor_tensor, nc.vector.tensor_scalar, nc.vector.scalar_tensor_tensor
            flat = lambda ap: ap.rearrange("p a b -> p (a b)")

            def lo(k, d=0):
                if isinstance(d, int) and k + 4 * d >= N_SLOTS:
                    return
                r = k % ROUND
                dve.wait_ge(hi_done, k + 4 * d + 1)
                tt(wlo[r][:, :], flat(raw[r][:, :, :]), whi[r][:, :].bitcast(F32), ALU.subtract).then_inc(lo_done, 1)

            def sums(tiles, b0, dest, n=2):
                for b in range(n):
                    dve.wait_ge(half_out, tiles + b + 1)
                    tt(dest(b), bank[b0 + b][:, 0:SEQ], xl[:, b, :], ALU.add).then_inc(tile_out, 1)

            def splits(k, d):
                for j in range(4):
                    lo(k + LEAD + j, d)

            def x_norm(m, l, gain):
                dve.wait_ge(root_x, m + 1)
                nc.vector.reciprocal(t1[:, :], t1[:, :]).then_inc(inv_x, 1)
                dve.wait_ge(inv_x, m + 1)

                def rest(j):
                    dve.wait_ge(h_hi, KT * m + j + 1)
                    tt(hT[:, j, 1, :], yo[:, j, :], hT[:, j, 0, :].bitcast(F32), ALU.subtract).then_inc(h_ready, 1)
                for j in range(KT):
                    stt(yo[:, j, :], xT[:, j, :], gain(j), t1[:, :], ALU.mult, ALU.mult).then_inc(h_f, 1)
                    if j >= 2:
                        rest(j - 2)
                rest(KT - 2)
                rest(KT - 1)

            def y_norm(m, gain):
                dve.wait_ge(root_y, m + 1)
                nc.vector.reciprocal(rn[:, :], rn[:, :]).then_inc(inv_y, 1)
                dve.wait_ge(inv_y, m + 1)

                def add(j):
                    dve.wait_ge(scaled_y, KT * m + j + 1)
                    tt(xT[:, j, :], xT[:, j, :], yo[:, j, :], ALU.add).then_inc(step_y, 1)
                for j in range(KT):
                    stt(yo[:, j, :], yo[:, j, :], gain(j), rn[:, :], ALU.mult, ALU.mult).then_inc(scaled_y, 1)
                    if j:
                        add(j - 1)
                add(KT - 1)
                dve.wait_ge(step_y, KT * (m + 1))

            def gain(l, which):
                return lambda j: prm[:, 2, 64 * l + 16 * which + j:64 * l + 16 * which + j + 1]

            def mixer(l, i, n, tiles, step, finish):
                V = n + 1
                col = lambda c: prm[:, l, bass.ds(c + i, 1)]
                der = lambda c: drv[:, l, bass.ds(c + i, 1)]
                dve.wait_ge(e["pair_done"], V)
                dve.wait_ge(tile_out, tiles)
                dve.wait_ge(e["diffed"], V)
                for j in range(3):
                    stt(sh[:, j, :], dsh[:, j, :], col(MU + PAIRS * j), zt[:, j, 1:], ALU.mult,
                        ALU.add).then_inc(e["shifted"], 1)
                dve.wait_ge(e["w_tanh"], V)
                ts(ldc[:, :, 1:], eN[:, :, :], -DECAY_C, -DECAY_C, ALU.mult, ALU.add).then_inc(e["ld_ready"], 1)
                dve.wait_ge(e["ld_ready"], V)
                nc.vector.tensor_tensor_scan(flat(cs[:, :, :]), hp, flat(ldc[:, :, :]), 0.0, ALU.mult,
                                             ALU.add).then_inc(e["cum_ready"], 1)
                step(0)
                if l:
                    dve.wait_ge(e["v_tanh"], V - PAIRS)
                    ts(kf[:, :], kf[:, :], 0.5, 0.5, ALU.mult, ALU.add).then_inc(e["v_gate"], 1)
                    dve.wait_ge(e["shifted"], 3 * n + 3)
                    tt(yf[:, :].unsqueeze(1), vf[:, bass.ds(i, 1), :], sh[:, 2:3, :],
                       ALU.subtract).then_inc(e["v_diff"], 1)
                    dve.wait_ge(e["v_gate"], V - PAIRS)
                    dve.wait_ge(e["v_diff"], V - PAIRS)
                    tt(yf[:, :], yf[:, :], kf[:, :], ALU.mult).then_inc(e["v_gated"], 1)
                    dve.wait_ge(e["v_gated"], V - PAIRS)
                    tt(sh[:, 2, :], sh[:, 2, :], yf[:, :], ALU.add).then_inc(e["v_ready"], 1)
                dve.wait_ge(e["a_tanh"], V)
                ts(kf[:, :], ta[:, :], der(HKA), der(OMKA), ALU.mult, ALU.add).then_inc(e["kf_ready"], 1)
                ts(ta[:, :], ta[:, :], -0.5, -0.5, ALU.mult, ALU.add).then_inc(e["af_ready"], 1)
                dve.wait_ge(e["kf_ready"], V)
                dve.wait_ge(e["shifted"], 3 * n + 3)
                tt(kf[:, :], sh[:, 1, :], kf[:, :], ALU.mult).then_inc(e["k2_ready"], 1)
                dve.wait_ge(e["k2_ready"], V)
                stt(t1[:, :], sh[:, 0, :], col(RK), kf[:, :], ALU.mult, ALU.mult).then_inc(e["t1_ready"], 1)
                dve.wait_ge(e["n2_root"], V)
                ts(rn[:, :], rn[:, :], 1e-12, None, ALU.max).then_inc(e["n2_max"], 1)
                dve.wait_ge(e["n2_max"], V)
                nc.vector.reciprocal(rn[:, :], rn[:, :]).then_inc(e["n2_inv"], 1)
                dve.wait_ge(e["n2_inv"], V)
                stt(rn[:, :], sh[:, 1, :], der(NKK), rn[:, :], ALU.mult, ALU.mult).then_inc(e["kk_ready"], 1)
                dve.wait_ge(e["kk_ready"], V)
                dve.wait_ge(e["af_ready"], V)
                tt(ta[:, :], rn[:, :], ta[:, :], ALU.mult).then_inc(e["b_ready"], 1)
                ch = lambda ap: ap.rearrange("p (u c t) -> p u c t", u=2, t=CHUNK)
                half = lambda j: AR[:, :, j, :].rearrange("p u (c t) -> p u c t", t=CHUNK)
                by_u = lambda ap: ap.rearrange("p (u c) t -> p u c t", u=2)
                dve.wait_ge(e["e_pos"], V)
                for u in range(2):
                    c4 = slice(2 * u, 2 * u + 2)
                    cc = lambda ap: ap.rearrange("p (c t) -> p c t", t=CHUNK)
                    toks = slice(P * u, P * u + P)
                    tt(cc(AR[:, u, 0, :]), cc(rn[:, toks]), eP[:, c4, 0:CHUNK], ALU.mult)
                    tt(cc(AR[:, u, 1, :]), cc(sh[:, 0, toks]), eP[:, c4, 1:], ALU.mult).then_inc(e["scaled"], 1)
                dve.wait_ge(e["e_neg"], V)
                tt(flat(ktl[:, :, :]), kf[:, :], flat(eN[:, :, :]), ALU.mult).then_inc(e["scaled"], 1)
                dve.wait_ge(e["b_ready"], V)
                tt(flat(btl[:, :, :]), ta[:, :], flat(eN[:, :, :]), ALU.mult).then_inc(e["scaled"], 1)
                step(1)
                dve.wait_ge(e["bonus_sum"], V)
                if l:
                    dve.wait_ge(e["v_ready"], V - PAIRS)
                tt(t1[:, :], mb[3][:, SEQ:2 * SEQ], sh[:, 2, :], ALU.mult).then_inc(e["bonus_ready"], 1)
                qk = zt[:, 3:5, 1:]
                tt(qr[:, :, :], qk, cst[:, C_COS:C_COS + SEQ].unsqueeze(1).to_broadcast([P, 2, SEQ]),
                   ALU.mult).then_inc(e["roped_c"], 1)
                dve.wait_ge(e["swapped"], 2 * n + 2)
                tt(xs[:, :, :], xs[:, :, :], cst[:, C_SIN:C_SIN + SEQ].unsqueeze(1).to_broadcast([P, 2, SEQ]),
                   ALU.mult).then_inc(e["roped_s"], 1)
                dve.wait_ge(e["roped_c"], V)
                dve.wait_ge(e["roped_s"], V)
                tt(qr[:, :, :], qr[:, :, :], xs[:, :, :], ALU.add).then_inc(e["roped"], 1)
                step(2)
                for unit in range(4):
                    dve.wait_ge(e["gram_sum"], 4 * n + unit + 1)
                    tt(G[:, unit, :, :].rearrange("p a b -> p (a b)"), mb[(unit + 2) % 4][:, :],
                       cst[:, C_GRAM:C_GRAM + 512], ALU.mult).then_inc(e["gram_ready"], 1)
                step(3)
                wait_alone(dve, e["tt_reset"], 8 * n + 8)
                wait_alone(dve, e["n_turned"], V)
                wait_alone(dve, e["gram_ready"], 4 * n + 4)
                for w in range(2):
                    us = slice(2 * w, 2 * w + 2)
                    m0 = lambda j: lvl[:, 0, j, :].unsqueeze(1).to_broadcast([P, 2, P])
                    nc.vector.copy_predicated(TT[:, us, 0, :], m0(0),
                                              mb[2][:, 256 * w:256 * w + 256].rearrange("p (a b) -> p a b", a=2))
                    nc.vector.copy_predicated(TT[:, us, 1, :], m0(1), G[:, us, 2, :]).then_inc(e["level_done"], 1)
                for lv in range(1, LEVELS):
                    for w in range(2):
                        us = slice(2 * w, 2 * w + 2)
                        wait_alone(dve, e["t_sum"], 2 * (LEVELS - 1) * n + 2 * lv - 1 + w)
                        new = mb[w][:, :].rearrange("p (a g b) -> p a g b", a=2, g=2)
                        if lv < LEVELS - 1:
                            nc.vector.copy_predicated(
                                TT[:, us, :, :].rearrange("p a g b -> p a (g b)"),
                                lvl[:, lv, :, :].rearrange("p g b -> p (g b)").unsqueeze(1).to_broadcast([P, 2, 256]),
                                mb[w][:, :].rearrange("p (a b) -> p a b", a=2)).then_inc(e["level_done"], 1)
                        else:
                            nc.vector.copy_predicated(
                                TT[:, us, 1, :], lvl[:, lv, 1, :].unsqueeze(1).to_broadcast([P, 2, P]),
                                new[:, :, 1, :]).then_inc(e["level_done"], 1)
                    step(3 + lv)
                    if lv == 1:
                        finish(0)
                dve.wait_ge(e["akv_out"], V)
                dve.wait_ge(e["e_chunk"], V)
                for c in range(NCH):
                    u, rows = c // 2, slice(CHUNK * (c % 2), CHUNK * (c % 2) + CHUNK)
                    if c:
                        dve.wait_ge(e["r_sum"], (NCH - 1) * n + c)
                        tt(Rb[rows, u, :], mb[0][rows, 0:P], AKV[rows, u, :], ALU.add).then_inc(e["r_out"], 1)
                    if c < NCH - 1:
                        dve.wait_ge(e["s_sum"], (NCH - 1) * n + c + 1)
                        stt(Stmp, mb[2][:, 0:P], eC[:, c:c + 1], blk, ALU.mult,
                            ALU.mult).then_inc(e["s_tmp"], 1)
                        dve.wait_ge(e["s_tmp"], (NCH - 1) * n + c + 1)
                        stt(St[:, c + 1, :], St[:, c, :], eC[:, c:c + 1], Stmp, ALU.mult,
                            ALU.add).then_inc(e["s_out"], 1)
                        if c < NCH - 2:
                            dve.wait_ge(e["s_out"], (NCH - 1) * n + c + 1)
                    if c == 0:
                        finish(1)
                    if c == 2:
                        step(9)
                ys = mb[3][:, 0:256].rearrange("p (a b) -> p a b", b=HEAD)
                y4 = flat(yn[:, :, :]).rearrange("p (a b) -> p a b", b=HEAD)
                wide = lambda ap: ap.unsqueeze(2).to_broadcast([P, 4, HEAD])
                dve.wait_ge(e["y_sum"], 2 * n + 2)
                nc.vector.tensor_reduce(small[:, 0:4], ys, AX.X, ALU.add).then_inc(e["y_mean"], 1)
                dve.wait_ge(e["y_mean"], 2 * n + 1)
                ts(small[:, 0:4], small[:, 0:4], 1.0 / HEAD, None, ALU.mult).then_inc(e["y_mean"], 1)
                dve.wait_ge(e["y_mean"], 2 * n + 2)
                tt(y4, ys, wide(small[:, 0:4]), ALU.subtract).then_inc(e["y_cen"], 1)
                dve.wait_ge(e["score_sum"], V)
                tt(sm[:, :], mb[2][:, 0:384], cst[:, C_CAUS:C_CAUS + 384], ALU.add).then_inc(e["masked"], 1)
                dve.wait_ge(e["masked"], V)
                nc.vector.tensor_reduce(small[:, 8:9], sm[:, 0:P], AX.X, ALU.max)
                nc.vector.tensor_reduce(small[:, 9:10], sm[:, P:3 * P], AX.X, ALU.max).then_inc(e["smax"], 1)
                dve.wait_ge(e["smax"], V)
                ts(small[:, 10:12], small[:, 8:10], -SCALE, None, ALU.mult).then_inc(e["nmax"], 1)
                dve.wait_ge(e["y_sq"], V)
                nc.vector.tensor_reduce(small[:, 4:8], flat(ysq[:, :, :]).rearrange("p (a b) -> p a b", b=HEAD),
                                        AX.X, ALU.add).then_inc(e["y_var"], 1)
                step(10)
                dve.wait_ge(e["y_root"], V)
                nc.vector.reciprocal(small[:, 4:8], small[:, 4:8]).then_inc(e["y_rinv"], 1)
                dve.wait_ge(e["y_rinv"], V)
                tt(y4, y4, wide(small[:, 4:8]), ALU.mult).then_inc(e["y_norm"], 1)
                dve.wait_ge(e["expd"], 2 * n + 2)
                nc.vector.reciprocal(small[:, 14:16], small[:, 12:14]).then_inc(e["rsum"], 1)
                dve.wait_ge(e["rsum"], V)
                ts(sm[:, 0:P], sm[:, 0:P], small[:, 14:15], None, ALU.mult)
                ts(sm[:, P:3 * P], sm[:, P:3 * P], small[:, 15:16], None, ALU.mult).then_inc(e["probs"], 1)
                dve.wait_ge(e["y_turned"], V)
                ts(yf[:, :], mb[0][:, 0:SEQ], col(LG), col(LB), ALU.mult, ALU.add).then_inc(e["y_gain"], 1)
                dve.wait_ge(e["y_gain"], V)
                dve.wait_ge(e["bonus_ready"], V)
                tt(yf[:, :], yf[:, :], t1[:, :], ALU.add).then_inc(e["y_bonus"], 1)
                dve.wait_ge(e["y_bonus"], V)
                dve.wait_ge(e["g_out"], V)
                tt(yf[:, :], yf[:, :], gs[:, :], ALU.mult).then_inc(e["y_gated"], 1)
                step(11)
                dve.wait_ge(e["y_hi"], V)
                tt(mT[:, bass.ds(i, 1), 1, :], yf[:, :].unsqueeze(1), mT[:, bass.ds(i, 1), 0, :].bitcast(F32),
                   ALU.subtract).then_inc(e["y_lo"], 1)
                if l == 0:
                    dve.wait_ge(e["v_kept"], V)
                dve.wait_ge(e["o_hi"], V)
                tt(mT[:, bass.ds(PAIRS + i, 1), 1, :], mb[1][:, 0:256].unsqueeze(1),
                   mT[:, bass.ds(PAIRS + i, 1), 0, :].bitcast(F32), ALU.subtract).then_inc(e["pair_done"], 1)
                finish(2)

            dve.wait_ge(const_in, 64)
            for j, place in enumerate((qr, xs, xl)):
                nc.vector.tensor_copy(lvl[:, 2 * j:2 * j + 2, :, :].rearrange("p a b c -> p (a b c)"),
                                      flat(place[:, :, :])).then_inc(lvl_ready, 1)
            dve.wait_ge(lvl_ready, 3)
            dve.wait_ge(prm_turned, 1)
            nc.vector.tensor_copy(flat(prm[:, :, :]), mb[3][:, 0:384]).then_inc(prm_ready, 1)
            dve.wait_ge(prm_ready, 1)
            for l in range(DEPTH):
                pl = lambda c, n=8: prm[:, l, c:c + n]
                ts(drv[:, l, HALF:HALF + 24], pl(W0, 24), 0.5, None, ALU.mult)
                ts(drv[:, l, HKA:HKA + 8], pl(KA), 0.5, None, ALU.mult)
                ts(drv[:, l, OMKA:OMKA + 8], pl(KA), -0.5, 1.0, ALU.mult, ALU.add)
                ts(drv[:, l, NKK:NKK + 8], pl(KK), -1.0, None, ALU.mult).then_inc(drv_ready, 1)
            for b8 in range(8):
                dve.wait_ge(x_turned, b8 + 1)
                nc.vector.tensor_copy(flat(xT[:, 2 * b8:2 * b8 + 2, :]), (bank + mb)[b8][:, :]).then_inc(x_ready, 1)
            dve.wait_ge(x_ready, 8)
            dve.wait_ge(clears, 2)
            for j in range(LEAD):
                lo(j)
            for l in range(DEPTH):
                x_norm(2 * l, l, gain(l, 0))
                k, t = start[l, "lora"]
                splits(k, 0)
                sums(t, 0, lambda b: zt[:, 3 + b, 1:])
                if l:
                    k, t = start[l, "vres"]
                    lo(k + LEAD)
                    sums(t, 2, lambda b: zt[:, 5, 1:], 1)
                t_all = start[l, "pairs"][1]
                dve.wait_ge(tile_out, t_all)
                for j in range(2 + l):
                    rows = slice(0, P if j < 2 else VRES)
                    tt(lact[rows, j, :], zt[rows, 3 + j, 0:SEQ], zt[rows, 3 + j, 1:], ALU.subtract).then_inc(l_diff, 1)
                    dve.wait_ge(l_diff, 2 * l + j + 1)
                    mu = prm[rows, l, MU + 24 + j:MU + 25 + j]
                    stt(lact[rows, j, :], lact[rows, j, :], mu, zt[rows, 3 + j, 1:], ALU.mult,
                        ALU.add).then_inc(l_shift, 1)
                dve.wait_ge(l_tanh, 2 * l + 2)
                ts(lact[:, 1, :], lact[:, 1, :], 0.5, 0.5, ALU.mult, ALU.add).then_inc(l_ready, 1)
                k, t = start[l, "pairs"]

                def place(g):
                    return lambda b: zt[:, 2 * g + b, 1:]
                for g in range(3):
                    splits(k + 4 * g, 0)
                    sums(t + 2 * g, 2 * (1 - g % 2), place(g))

                def turn(i):
                    def finish(g):
                        sums(t + 6 + 2 * g + i * 6, 2 * (1 - g % 2), place(g))
                    mixer(l, i, PAIRS * l + i, t + 6 + i * 6, lambda j: lo(k + 12 + j + LEAD, i * 3), finish)
                loop(dve, PAIRS - 1, turn)
                mixer(l, PAIRS - 1, PAIRS * l + PAIRS - 1, t + 6 * PAIRS, lambda j: None, lambda g: None)
                k, t = start[l, "out"]

                def turn(i):
                    for g in range(2):
                        splits(k + 4 * g, i * 2)
                        sums(t + 2 * g + i * 4, 2 * g,
                             lambda b: yo[:, bass.ds(i * 4 + 2 * g + b, 1), :].rearrange("p a b -> p (a b)"))
                loop(dve, 4, turn)
                y_norm(2 * l, gain(l, 1))
                x_norm(2 * l + 1, l, gain(l, 2))
                k, t = start[l, "mlp"]
                for q0, nq, last in runs(l):
                    def quarter(q):
                        qq = q + q0

                        def up_turn(i):
                            for g in range(2):
                                splits(k + 4 * g, qq * 16 + i * 2)
                                T = t + 2 * g + qq * 32 + i * 4
                                M = 64 * l + 2 * g + qq * 16 + i * 4
                                hid = lambda b: AR[:, b, :, :].rearrange("p a b -> p (a b)")
                                for b in range(2):
                                    dve.wait_ge(half_out, T + b + 1)
                                    tt(hid(b), bank[2 * g + b][:, 0:SEQ], xl[:, b, :], ALU.add).then_inc(up_sum, 1)
                                for b in range(2):
                                    dve.wait_ge(up_sum, M + b + 1)
                                    stt(hid(b), hid(b), 0.0, hid(b), ALU.max, ALU.mult).then_inc(up_relu, 1)
                                for b in range(2):
                                    dve.wait_ge(up_hi, M + b + 1)
                                    at = bass.ds(i * 4 + 2 * g + b, 1)
                                    tt(mT[:, at, 1, :], hid(b).unsqueeze(1), mT[:, at, 0, :].bitcast(F32),
                                       ALU.subtract).then_inc(tile_out, 1)
                        loop(dve, 4, up_turn)

                        def down_turn(i):
                            for g in range(2):
                                splits(k + 32 + 4 * g, qq * 16 + i * 2)
                                T = t + 16 + 2 * g + qq * 32 + i * 4
                                M = 64 * l + 2 * g + qq * 16 + i * 4
                                for b in range(2):
                                    dve.wait_ge(half_out, T + b + 1)
                                    tt(xl[:, b, :], bank[2 * g + b][:, 0:SEQ], xl[:, b, :],
                                       ALU.add).then_inc(down_sum, 1)
                                for b in range(2):
                                    dve.wait_ge(down_sum, M + b + 1)
                                    at = bass.ds(i * 4 + 2 * g + b, 1)
                                    tt(yo[:, at, :], yo[:, at, :], xl[:, b, :].unsqueeze(1),
                                       ALU.add).then_inc(tile_out, 1)
                        dve.wait_ge(clears, 3 + l)
                        loop(dve, 3 if last else 4, down_turn)
                        if last:
                            down_turn(3)
                    loop(dve, nq, quarter)
                y_norm(2 * l + 1, gain(l, 3))
            for b8 in range(8):
                dve.wait_ge(out_turned, b8 + 1)
                u, tile = b8 // 4, 4 * (b8 % 4)
                at = (16 * u + tile) * P
                nc.vector.tensor_copy(yof[:, at:at + 512], (bank + mb)[b8][:, :]).then_inc(out_copied, 1)


_INS = ["x", "norm_mix_pre", "norm_mix_post", "norm_mlp_pre", "norm_mlp_post", "w_in", "w_in_vres", "shift_mu",
        "shift_mu_vres", "decay_w0", "decay_w2", "iclr_a0", "iclr_a2", "vres_v0", "vres_v2", "gate_g2", "k_k", "k_a",
        "r_k", "lnx_gain", "lnx_bias", "w_out", "w_up", "w_down"]


def kernel(**inputs):
    import concourse.bacc as bacc
    from concourse.bass_utils import run_bass_kernel_spmd

    nc = bacc.Bacc("TRN2", target_bir_lowering=False, num_devices=1)
    consts, levels = shape_constants()
    arrays = {"in_consts": consts, "in_levels": levels}
    for name in _INS:
        arrays["in_" + name] = np.ascontiguousarray(inputs[name])
    args = [nc.dram_tensor(name, a.shape, mybir.dt.from_np(a.dtype), kind="ExternalInput").ap()
            for name, a in arrays.items()]
    out = nc.dram_tensor("out_0", (1, SEQ, D), F32, kind="ExternalOutput").ap()
    trunk(nc, *args, out)
    r = run_bass_kernel_spmd(nc, [arrays], core_ids=[0])
    return r.results[0]["out_0"]
```

```python
from contextlib import ExitStack

import numpy as np

import concourse.bass as bass
from concourse import mybir

F32 = mybir.dt.float32
F32R = mybir.dt.float32r
I8 = mybir.dt.uint8
ALU = mybir.AluOpType
ACT = mybir.ActivationFunctionType
AX = mybir.AxisListType

P = 128
SEQ = 256
D = 2048
DEPTH = 2
KT = D // P
C = 1024
HEAD = 64
PAIRS = C // P
N_SHIFT = 3 * C + 256
N_IN = N_SHIFT + 3 * C
FF = 4 * D
CHUNK = 64
NCH = SEQ // CHUNK
VRES = 32
DECAY_C = 0.5 * float(np.exp(-0.5))
SHIFT = DECAY_C * CHUNK
EPS = 1e-6
LNX_EPS = 64e-5
SCALE = P ** -0.5
LEVELS = 6
ROUND = 4
SK = 4
LEAD = 3
POOL_LO = (2, 5, 8, 11, 14)
POOL_TILES = tuple(j for j in range(KT) if j % 3 != 2)
Y_SUMMED = KT - 2
OUT_TILES = ((0, 1, 2, 3), (8, 9, 10, 11), (4, 5, 12, 13), (6, 7, 14, 15))
OUT_ORDER = ((0, 0), (0, 1), (0, 2), (1, 0), (1, 1), (1, 2), (0, 3), (1, 3))

MU, MU_V, W0, A0, V0, KK, KA, RK, LG, LB, NPRM = 0, 26, 27, 35, 43, 51, 59, 67, 75, 83, 91
HALF, HKA, OMKA, NKK, KK2, NDRV = 0, 24, 32, 40, 48, 56
C_ID, C_BLK, C_ONE, C_COL, C_GRAM, C_CAUS, C_COS, C_SIN, C_SCAN = 0, 128, 256, 384, 388, 900, 1284, 1540, 1796
NCONST = C_SCAN + NCH * (CHUNK + 1)
NFIRST = C_GRAM


def shape_constants():
    c = np.zeros((P, NCONST), np.float32)
    row, col = np.arange(P)[:, None], np.arange(P)[None, :]
    c[:, C_ID:C_ID + P] = row == col
    c[:, C_BLK:C_BLK + P] = row // HEAD == col // HEAD
    c[:, C_ONE:C_ONE + P] = 1
    same = row // CHUNK == col // CHUNK
    strict, incl = same & (row < col), same & (row <= col)
    c[:, C_GRAM:C_GRAM + 512] = np.concatenate([strict, incl, strict, incl], 1)
    tri = np.where(row <= col, 0, -1e30).T
    c[:, C_CAUS:C_CAUS + 384] = np.concatenate([tri, np.zeros((P, P)), tri], 1)
    half = P // 2
    freq = np.float32(10000.0) ** (-np.arange(half, dtype=np.float32) / np.float32(half))
    ang = freq[:, None] * np.arange(SEQ, dtype=np.float32)[None, :]
    c[:, C_COS:C_COS + SEQ] = np.concatenate([np.cos(ang), np.cos(ang)], 0)
    c[:, C_SIN:C_SIN + SEQ] = np.concatenate([-np.sin(ang), np.sin(ang)], 0)
    scan = np.ones((P, NCH, CHUNK + 1), np.float32)
    scan[:, :, 0] = 0
    c[:, C_SCAN:C_SCAN + NCH * (CHUNK + 1)] = scan.reshape(P, -1)
    c[:, C_COL:C_COL + 4] = [SHIFT, -SHIFT, EPS, LNX_EPS]
    levels = np.zeros((P, LEVELS, 2, P // 2), np.float32)
    for l in range(LEVELS):
        b = 1 << l
        low = (row // (2 * b) == col // (2 * b)) & (row // b % 2 == 1) & (col // b % 2 == 0)
        levels[:, l, 0] = low[:, np.arange(P) // b % 2 == 0]
        levels[:, l, 1] = low.T[:, np.arange(P) // b % 2 == 1]
    return c, levels.reshape(P, -1)


def trunk(nc, consts, levels, x, norm_mix_pre, norm_mix_post, norm_mlp_pre, norm_mlp_post, w_in, w_in_vres,
          shift_mu, shift_mu_vres, decay_w0, decay_w2, iclr_a0, iclr_a2, vres_v0, vres_v2,
          gate_g2, k_k, k_a, r_k, lnx_gain, lnx_bias, w_out, w_up, w_down, out):
    with ExitStack() as ctx:
        def sb(name, shape, dt=F32):
            return ctx.enter_context(nc.sbuf_tensor("b_" + name, shape, dt))

        def sem(name):
            return ctx.enter_context(nc.semaphore(name))

        bank = [ctx.enter_context(nc.psum_tensor(f"gemm_bank{i}", [P, 512], F32)) for i in range(4)]
        mb = [ctx.enter_context(nc.psum_tensor(f"mix_bank{i}", [P, 512], F32)) for i in range(4)]

        raw = [sb(f"raw{i}", [P, SK, 256]) for i in range(ROUND)]
        whi = [sb(f"whi{i}", [P, SK * 256], F32R) for i in range(ROUND)]
        wlo = [sb(f"wlo{i}", [P, SK * 256], F32R) for i in range(ROUND)]
        xT = sb("xT", [P, KT, SEQ])
        hT = sb("hT", [P, KT, 2, SEQ], F32R)
        mT = sb("mT", [P, KT, 2, SEQ], F32R)
        yo = sb("yo", [P, KT, SEQ])
        xl = sb("xl", [P, 2, SEQ])
        vf = sb("vf", [P, PAIRS, SEQ])
        prm = sb("prm", [P, 3, P])
        drv = sb("drv", [P, DEPTH, NDRV])
        cst = sb("cst", [P, NCONST])
        lvl = sb("lvl", [P, LEVELS, 2, P // 2], I8)
        lact = sb("lact", [P, 3, SEQ])
        lw = sb("lw", [P, 3, P])
        zt = sb("zt", [P, 6, SEQ + 1])
        sh = sb("sh", [P, 3, SEQ])
        rn = sb("rn", [P, SEQ])
        t1 = sb("t1", [P, SEQ])
        ldc = sb("ldc", [P, NCH, CHUNK + 1])
        cs = sb("cs", [P, NCH, CHUNK + 1])
        eP = sb("eP", [P, NCH, CHUNK + 1])
        eN = sb("eN", [P, NCH, CHUNK])
        eC = sb("eC", [P, NCH])
        ta = sb("ta", [P, SEQ])
        kf = sb("kf", [P, SEQ])
        AR = sb("AR", [P, 2, 2, P])
        ktl = sb("ktl", [P, 2, P])
        btl = sb("btl", [P, 2, P])
        tm = sb("tm", [P, 2, 3, P])
        AKV = sb("AKV", [P, 2, P])
        Rb = sb("Rb", [P, 2, P])
        U = sb("U", [P, 2, P])
        St = sb("St", [P, NCH, P])
        yn = sb("yn", [P, 2, P])
        ysq = Rb
        yf = sb("yf", [P, SEQ])
        gs = sb("gs", [P, SEQ])
        small = sb("small", [P, 16])
        spare = sb("spare", [P, 1])
        qr = sb("qr", [P, 2, SEQ])
        xs = sb("xs", [P, 2, SEQ])
        sm = sb("sm", [P, 384])
        vt = AKV
        Stmp = yf[:, 0:P]
        yof = yo[:, :, :].rearrange("p a b -> p (a b)")
        G = yof[:, 0:2048].rearrange("p (n g t) -> p n g t", n=4, g=4)
        TT = yof[:, 2048:3072].rearrange("p (n g t) -> p n g t", n=4, g=2)
        X = yof[:, 3072:3584].rearrange("p (n t) -> p n t", n=4)
        pt = yof[:, 3584:3968]
        ident = cst[:, C_ID:C_ID + P]
        blk = cst[:, C_BLK:C_BLK + P]
        ones = cst[:, C_ONE:C_ONE + P]
        col_shift, col_nshift = cst[:, C_COL:C_COL + 1], cst[:, C_COL + 1:C_COL + 2]
        col_eps, col_lnx = cst[:, C_COL + 2:C_COL + 3], cst[:, C_COL + 3:C_COL + 4]
        dsh = yof[:, 3072:3072 + 3 * SEQ].rearrange("p (a b) -> p a b", b=SEQ)
        hp = cst[:, C_SCAN:C_SCAN + NCH * (CHUNK + 1)]

        landed = [sem(f"slot{i}_landed") for i in range(ROUND)]
        hi_done = sem("hi_done")
        lo_done = sem("lo_done")
        slot_used = sem("slot_used")
        half_out = sem("half_out")
        tile_out = sem("tile_out")
        up_sum = sem("up_sum")
        up_relu = sem("up_relu")
        up_hi = sem("up_hi")
        first_in, const_in, gain_in, prm_in = sem("first_in"), sem("const_in"), sem("gain_in"), sem("prm_in")
        x_in = [sem("x_in_lower"), sem("x_in_upper")]
        stage_clear, lvl_ready = sem("stage_clear"), sem("lvl_ready")
        clears = sem("clears")
        gain_turned, gain_ready = sem("gain_turned"), sem("gain_ready")
        prm_turned, prm_ready, drv_ready = sem("prm_turned"), sem("prm_ready"), sem("drv_ready")
        x_turned, x_ready = sem("x_turned"), sem("x_ready")
        sq_y, sum_y, root_y, inv_y = sem("sq_y"), sem("sum_y"), sem("root_y"), sem("inv_y")
        acc_clear, used_y, scaled_y, down_sum = sem("acc_clear"), sem("used_y"), sem("scaled_y"), sem("down_sum")
        step_y = [sem("step_y_vector"), sem("step_y_pool")]
        sq_x, root_x, inv_x, used_x = sem("sq_x"), sem("root_x"), sem("inv_x"), sem("used_x")
        h_f, h_hi = sem("h_f"), sem("h_hi")
        h_ready = [sem("h_ready_vector"), sem("h_ready_pool")]
        out_turned, out_copied, stored = sem("out_turned"), sem("out_copied"), sem("stored")
        l_diff, l_shift, l_tanh, l_ready = sem("l_diff"), sem("l_shift"), sem("l_tanh"), sem("l_ready")
        names = ["lw_in", "pair_done", "diffed", "shifted", "v_kept", "kk_sq", "lora_w", "lora_a", "lora_g", "lora_v",
                 "w_tanh", "a_tanh", "g_out", "v_tanh", "ld_ready", "cum_ready", "e_pos", "e_neg", "e_chunk",
                 "kf_ready", "k2_ready", "af_ready", "v_gate", "v_diff", "v_gated", "v_ready",
                 "t1_ready", "n2_sum", "n2_root", "n2_max", "n2_inv", "kk_ready", "b_ready", "scaled",
                 "bonus_sum", "bonus_ready", "turned", "tm_ready", "gram_sum", "gram_ready", "tt_reset",
                 "n_turned", "level_done", "x_sum", "x_out", "t_sum", "akv_sum", "akv_out", "r_sum", "r_out",
                 "u_sum", "u_out", "s_sum", "s_tmp", "s_out", "y_sum", "y_mean", "y_cen", "y_sq", "y_var", "y_root",
                 "y_rinv", "y_norm", "y_turned", "y_gain", "y_bonus", "y_scaled", "y_gated", "y_hi", "x_free",
                 "swapped", "roped_c", "roped_s", "roped", "va_turned", "va_out", "score_sum", "masked", "smax",
                 "nmax", "expd", "rsum", "probs", "p_turned", "p_out", "o_sum", "o_hi", "o_lo"]
        e = {n: sem("m_" + n) for n in names}

        start = {}
        k = t = 0
        for l in range(DEPTH):
            for name, slots, tiles in (("lora", 4, 2), ("vres", l and 1, l and 1), ("pairs", 96, 48),
                                       ("out", 32, 16), ("mlp", 256, 128)):
                start[l, name] = (k, t)
                k, t = k + slots, t + tiles
        N_SLOTS = k

        def runs(l):
            return [(0, 3, False), (3, 1, True)]

        def taken(m, j, who):
            mine = [len(POOL_TILES), KT - len(POOL_TILES)][1 - who]
            return mine * m + sum((a in POOL_TILES) == bool(who) for a in range(j + 1))

        def tile_made(m, j):
            who = int(j in POOL_LO)
            per_norm = len(POOL_LO) if who else KT - len(POOL_LO)
            return h_ready[who], per_norm * m + sum((a in POOL_LO) == bool(who) for a in range(j + 1))

        def wait_alone(eng, semaphore, value):
            if not isinstance(value, int):
                value = eng.snap(eng.to_reg(value))
            eng.wait_ge(const_in, 48)
            eng.wait_ge(semaphore, value)

        def blocks(ap, lv, odd):
            dims = "p a" if len(ap.shape) == 3 else "p"
            ap = ap.rearrange(f"{dims} (n h b) -> {dims} n h b", h=2, b=1 << lv)
            return ap[:, :, :, odd, :] if dims == "p a" else ap[:, :, odd, :]

        def packed(ap, lv):
            dims = "p a" if len(ap.shape) == 3 else "p"
            return ap.rearrange(f"{dims} (n b) -> {dims} n b", b=1 << lv)

        def loop(eng, n, body):
            if n == 1:
                body(0)
            else:
                with eng.Fori(0, n) as i:
                    body(i)

        block = ctx.enter_context(nc.Block())

        @block.sync
        def _(sp):
            def fetch(k, d, parts):
                r = k % ROUND
                if not (isinstance(d, int) and k + 4 * d < ROUND):
                    sp.wait_ge(hi_done, k + 4 * d - ROUND + 1)
                    sp.wait_ge(lo_done, k + 4 * d - ROUND + 1)
                for a, b, src in parts:
                    sp.dma_start(raw[r][:, :, a:b], src).then_inc(landed[r], 32 // len(parts))

            def view(w):
                return w.rearrange("(kt p) n -> p kt n", p=P)

            def pair_group(l, k, d, i, g):
                w = view(w_in[l])
                a, b = ((0, C), (2 * C, N_SHIFT), (N_SHIFT + C, N_SHIFT + 2 * C))[g]
                for j in range(4):
                    kts = slice(SK * j, SK * j + SK)
                    fetch(k + j, d, [(0, P, w[:, kts, bass.ds(a + i * P, P)]),
                                     (P, 2 * P, w[:, kts, bass.ds(b + i * P, P)])])

            sp.dma_start(cst[:, 0:NFIRST], consts[:, 0:NFIRST]).then_inc(first_in, 16)
            yx = yo[:, :, :].rearrange("p a b -> p (a b)").rearrange("p (u f) -> p u f", u=2)
            for a in range(2):
                half = slice(a * D // 2, (a + 1) * D // 2)
                sp.dma_start(yx[:, :, half],
                             x[0].rearrange("(u p) f -> p u f", p=P)[:, :, half]).then_inc(x_in[a], 16)
            for j, g in enumerate((norm_mix_pre, norm_mix_post, norm_mlp_pre, norm_mlp_post)):
                sp.dma_start(tm[32 * j:32 * j + 32, 0, 2, :],
                             g.rearrange("l (a b) -> (l a) b", b=P)).then_inc(gain_in, 16)

            def late_constants():
                sp.dma_start(cst[:, NFIRST:], consts[:, NFIRST:]).then_inc(const_in, 16)
                for place, a, b in ((qr, 0, 4), (xs, 4, LEVELS)):
                    sp.dma_start(place[:, :, :].rearrange("p a b -> p (a b)")[:, 0:P * (b - a)],
                                 levels[:, P * a:P * b]).then_inc(const_in, 16)

            for l in range(DEPTH):
                w = view(w_in[l])
                k, t = start[l, "lora"]
                for j in range(4):
                    fetch(k + j, 0, [(0, 256, w[:, SK * j:SK * j + SK, 3 * C:3 * C + 256])])
                if l == 0:
                    late_constants()
                if l:
                    k, t = start[l, "vres"]
                    sp.wait_ge(hi_done, k - ROUND + 1)
                    sp.wait_ge(lo_done, k - ROUND + 1)
                    r = k % ROUND
                    sp.dma_start(raw[r][:, :, :].rearrange("p a b -> p (a b)")[:, 0:KT * VRES]
                                 .rearrange("p (kt n) -> p kt n", n=VRES),
                                 view(w_in_vres[l - 1])).then_inc(landed[r], 32)
                k, t = start[l, "pairs"]
                for g in range(2):
                    pair_group(l, k + 4 * g, 0, 0, g)

                def turn(i):
                    pair_group(l, k + 8, i * 3, i, 2)
                    for g in range(2):
                        pair_group(l, k + 12 + 4 * g, i * 3, i + 1, g)
                loop(sp, PAIRS - 1, turn)
                pair_group(l, k + 92, 0, PAIRS - 1, 2)
                k, t = start[l, "out"]
                w = view(w_out[l])
                for j, (g, s) in enumerate(OUT_ORDER):
                    r = (k + j) % ROUND
                    sp.wait_ge(hi_done, k + j - ROUND + 1)
                    sp.wait_ge(lo_done, k + j - ROUND + 1)
                    for at in (0, 2):
                        kt = OUT_TILES[s][at]
                        sp.dma_start(raw[r][:, at:at + 2, :],
                                     w[:, kt:kt + 2, 256 * g:256 * g + 256]).then_inc(landed[r], 16)

                def turn(i):
                    for j in range(8):
                        fetch(k + 8 + j, i * 2, [(0, 256, w[:, SK * (j % 4):SK * (j % 4) + SK,
                                                            bass.ds(i * 512 + 512 + 256 * (j // 4), 256)])])
                loop(sp, 3, turn)
                k, t = start[l, "mlp"]
                up, down = view(w_up[l]), view(w_down[l])
                for q0, nq, last in runs(l):
                    def quarter(q):
                        qq = q + q0

                        def up_turn(i):
                            for j in range(8):
                                fetch(k + j, qq * 16 + i * 2,
                                      [(0, 256, up[:, SK * (j % 4):SK * (j % 4) + SK,
                                                   bass.ds(qq * D + i * 512 + 256 * (j // 4), 256)])])
                        loop(sp, 4, up_turn)

                        def down_turn(i):
                            for j in range(8):
                                fetch(k + 32 + j, qq * 16 + i * 2,
                                      [(0, 256, down[:, bass.ds(qq * KT + SK * (j % 4), SK),
                                                     bass.ds(i * 512 + 256 * (j // 4), 256)])])
                        loop(sp, 4, down_turn)
                    loop(sp, nq, quarter)
            for q in range(4):
                for u in range(2):
                    sp.wait_ge(out_copied, 2 * q + u + 1)
                    sp.dma_start(out[0, P * u:P * u + P, 512 * q:512 * q + 512],
                                 raw[q][:, 2 * u:2 * u + 2, :].rearrange("p a b -> p (a b)")).then_inc(stored, 16)
            sp.wait_ge(stored, 8 * 16)

        @block.gpsimd
        def _(pool):
            stage = tm[:, :, :, :].rearrange("p a b c -> p (a b) c")
            nc.gpsimd.memset(stage[:, 0:2, :], 0.0).then_inc(stage_clear, 1)
            nc.gpsimd.memset(zt[:, :, 0:1], 0.0).then_inc(clears, 1)
            nc.gpsimd.memset(ldc[:, :, 0:1], 0.0).then_inc(e["x_free"], 1)
            nc.gpsimd.memset(St[:, 0, :], 0.0).then_inc(e["pair_done"], 1)
            pool.wait_ge(stage_clear, 1)
            for l in range(DEPTH):
                rows = [(MU, shift_mu[l], 26), (W0, decay_w0[l], 8), (A0, iclr_a0[l], 8), (KK, k_k[l], 8),
                        (KA, k_a[l], 8), (RK, r_k[l].rearrange("h d -> (h d)"), 8), (LG, lnx_gain[l], 8),
                        (LB, lnx_bias[l], 8)]
                if l:
                    rows.append((V0, vres_v0[l - 1], 8))
                for at, src, n in rows:
                    pool.dma_start(stage[at:at + n, l, :], src.rearrange("(a b) -> a b", b=P)).then_inc(prm_in, 16)
                if l:
                    pool.dma_start(stage[MU_V:MU_V + 1, l, 0:VRES],
                                   shift_mu_vres[l - 1:l, :]).then_inc(prm_in, 16)

            def pair_weights(l, i):
                cols = bass.ds(i * P, P)
                pool.dma_start(lw[0:64, 0, :], decay_w2[l][:, cols]).then_inc(e["lw_in"], 16)
                pool.dma_start(lw[64:128, 0, :], iclr_a2[l][:, cols]).then_inc(e["lw_in"], 16)
                pool.dma_start(lw[:, 1, :], gate_g2[l][:, cols]).then_inc(e["lw_in"], 16)
                if l:
                    pool.dma_start(lw[0:VRES, 2, :], vres_v2[l - 1][:, cols]).then_inc(e["lw_in"], 16)

            pair_weights(0, 0)

            def unit(l, i, n, tiles, slot, after):
                pool.wait_ge(tile_out, tiles - 2)
                pool.wait_ge(e["x_free"], n + 1)
                for j in (1, 0):
                    nc.gpsimd.tensor_tensor(dsh[:, j, :], zt[:, j, 0:SEQ], zt[:, j, 1:SEQ + 1],
                                            ALU.subtract).then_inc(e["diffed"], 1)
                for j in range(2):
                    pool.wait_ge(hi_done, slot + j + 1)
                    pool.wait_ge(lo_done, slot + j)
                    at = (start[l, "pairs"][0] + 9 + j) % ROUND
                    nc.gpsimd.tensor_tensor(wlo[at][:, :], raw[at][:, :, :].rearrange("p a b -> p (a b)"),
                                            whi[at][:, :].bitcast(F32), ALU.subtract).then_inc(lo_done, 1)
                pool.wait_ge(e["pair_done"], n + 1)
                pool.wait_ge(tile_out, tiles)
                nc.gpsimd.tensor_tensor(dsh[:, 2, :], zt[:, 2, 0:SEQ], zt[:, 2, 1:SEQ + 1],
                                        ALU.subtract).then_inc(e["diffed"], 1)
                if l:
                    pool.wait_ge(e["shifted"], 3 * n + 3)
                    nc.gpsimd.tensor_tensor(xs[:, 1:2, :], vf[:, bass.ds(i, 1), :], sh[:, 2:3, :],
                                            ALU.subtract).then_inc(e["v_diff"], 1)
                    pool.wait_ge(e["v_gate"], n + 1 - PAIRS)
                    pool.wait_ge(e["v_diff"], n + 1 - PAIRS)
                    nc.gpsimd.tensor_tensor(xs[:, 1, :], xs[:, 1, :], xs[:, 0, :], ALU.mult).then_inc(e["v_gated"], 1)
                    pool.wait_ge(e["v_gated"], n + 1 - PAIRS)
                    nc.gpsimd.tensor_tensor(sh[:, 2, :], sh[:, 2, :], xs[:, 1, :], ALU.add).then_inc(e["v_ready"], 1)
                pool.wait_ge(e["lora_g"], n + 1)
                if l:
                    pool.wait_ge(e["lora_v"], n + 1 - PAIRS)
                after()
                for a in range(4):
                    for b in range(2):
                        nc.gpsimd.tensor_copy(TT[:, a, b, :], ident).then_inc(e["tt_reset"], 1)
                if l == 0:
                    pool.wait_ge(e["shifted"], 3 * n + 3)
                    nc.gpsimd.tensor_copy(vf[:, bass.ds(i, 1), :], sh[:, 2:3, :]).then_inc(e["v_kept"], 1)

            def square_sum(m, a, i, n=4):
                for j in range(n):
                    pool.wait_ge(sq_y, KT * m + a + j + 1 + i * 4)
                    if a + j or not isinstance(i, int):
                        pool.wait_ge(used_y, Y_SUMMED * m + a + j + i * 4)
                    nc.gpsimd.tensor_tensor(gs[:, :], gs[:, :], zt[:, j, 1:], ALU.add).then_inc(used_y, 1)

            def take_in(m):
                for j in POOL_TILES:
                    pool.wait_ge(scaled_y, KT * m + j + 1)
                    nc.gpsimd.tensor_tensor(xT[:, j, :], xT[:, j, :], yo[:, j, :], ALU.add).then_inc(step_y[1], 1)

            def x_rest(m):
                for j in POOL_LO:
                    pool.wait_ge(h_hi, KT * m + j + 1)
                    nc.gpsimd.tensor_tensor(hT[:, j, 1, :], yo[:, j, :], hT[:, j, 0, :].bitcast(F32),
                                            ALU.subtract).then_inc(h_ready[1], 1)

            for l in range(DEPTH):
                x_rest(2 * l)
                k, t = start[l, "pairs"]
                loop(pool, PAIRS - 1, lambda i: unit(l, i, PAIRS * l + i, t + 4 + i * 6, k + 9 + i * 12,
                                                     lambda: pair_weights(l, i + 1)))
                unit(l, PAIRS - 1, PAIRS * l + PAIRS - 1, t + 6 * PAIRS - 2, k + 93,
                     lambda: pair_weights(l + 1, 0) if l < DEPTH - 1 else None)
                pool.wait_ge(e["pair_done"], PAIRS * (l + 1) + 1)
                nc.gpsimd.memset(gs[:, :], 0.0).then_inc(acc_clear, 1)
                pool.wait_ge(acc_clear, 2 * l + 1)
                square_sum(2 * l, 0, 0)
                loop(pool, 2, lambda i: square_sum(2 * l, 4, i))
                square_sum(2 * l, 12, 0, 2)
                take_in(2 * l)
                x_rest(2 * l + 1)
                for j in (POOL_LO[-1], KT - 1):
                    pool.wait_ge(*tile_made(2 * l + 1, j))
                nc.gpsimd.memset(yof, 0.0).then_inc(clears, 1)
                nc.gpsimd.memset(gs[:, :], 0.0).then_inc(acc_clear, 1)
                pool.wait_ge(acc_clear, 2 * l + 2)
                loop(pool, 3, lambda i: square_sum(2 * l + 1, 0, i))
                square_sum(2 * l + 1, 12, 0, 2)
                take_in(2 * l + 1)

        @block.tensor
        def _(pe):
            mm, turned = nc.tensor.matmul, nc.tensor.transpose

            def tick(k, d, j, act, kt, b0, first, last, first_j=0, last_j=SK - 1):
                r = k % ROUND
                if j == first_j:
                    pe.wait_ge(hi_done, k + 4 * d + 1)
                    pe.wait_ge(lo_done, k + 4 * d + 1)
                pair = act[:, kt, :, :].rearrange("p a b -> p (a b)")
                for b in range(2):
                    cols = slice(256 * j + P * b, 256 * j + P * b + P)
                    if not last:
                        mm(bank[b0 + b][:, :], whi[r][:, cols], pair, start=first, stop=False)
                    m = mm(bank[b0 + b][:, 0:SEQ], wlo[r][:, cols], act[:, kt, 0, :], start=False, stop=False)
                    if last:
                        m = mm(bank[b0 + b][:, :], whi[r][:, cols], pair, start=False, stop=True)
                if j == last_j:
                    m.then_inc(slot_used, 1)

            def group(k, d, tiles, act, b0, made=lambda kt: None):
                if not (isinstance(tiles, int) and tiles <= 0):
                    pe.wait_ge(tile_out, tiles)
                for kt in range(KT):
                    if made(kt):
                        pe.wait_ge(*made(kt))
                    tick(k + kt // SK, d, kt % SK, act, kt, b0, kt == 0, kt == KT - 1)

            def pair_ticks(a, b, k, d, tiles):
                for x in range(a, b):
                    g, kt = x // KT, x % KT
                    if kt == 0:
                        pe.wait_ge(tile_out, tiles + 2 * (g == 2))
                    tick(k + x // SK, d, x % SK, hT, kt, (2, 0, 2)[g], kt == 0, kt == KT - 1)

            def last_ticks(a, b, k, tiles):
                for x in range(a, b):
                    if x < KT:
                        pair_ticks(x, x + 1, k, 0, tiles)
                        continue
                    g, s = OUT_ORDER[(x - KT) // SK]
                    if x in (16, 28):
                        pe.wait_ge(tile_out, tiles + 2 * g)
                    tick(k + x // SK, 0, x % SK, mT, OUT_TILES[s][x % SK], 2 * g, x in (16, 28), False)

            def x_sum(m):
                for j in range(KT):
                    pe.wait_ge(sq_x, KT * m + j + 1)
                    mm(mb[0][:, 0:SEQ], ones, sh[:, j % 3, :], start=j == 0, stop=j == KT - 1).then_inc(used_x, 1)

            def y_sum(m):
                pe.wait_ge(used_y, Y_SUMMED * (m + 1))
                mm(mb[0][:, 0:SEQ], ones, gs[:, :], start=True, stop=False)
                for j in (Y_SUMMED, Y_SUMMED + 1):
                    pe.wait_ge(sq_y, KT * m + j + 1)
                    mm_j = mm(mb[0][:, 0:SEQ], ones, zt[:, j % 4, 1:], start=False, stop=j == KT - 1)
                mm_j.then_inc(sum_y, 1)

            pe.wait_ge(first_in, 16)
            yx = yof.rearrange("p (u f) -> p u f", u=2)
            for b8 in range(8):
                bk = (bank + mb)[b8]
                pe.wait_ge(x_in[b8 // 4], 16)
                for q in range(2):
                    for u in range(2):
                        j = 2 * b8 + q
                        m = turned(bk[:, 256 * q + P * u:256 * q + P * u + P], yx[:, u, P * j:P * j + P], ident)
                m.then_inc(x_turned, 1)
            stage = tm[:, :, :, :].rearrange("p a b c -> p (a b) c")
            pe.wait_ge(gain_in, 64)
            pe.wait_ge(x_ready, 8)
            turned(mb[1][:, 0:P], stage[:, 2, :], ident).then_inc(gain_turned, 1)

            def key_norms(n):
                pe.wait_ge(e["kk_sq"], n + 1)
                mm(mb[0][:, SEQ:2 * SEQ], blk, rn[:, :], start=True, stop=True).then_inc(e["n2_sum"], 1)

            def mixer(l, i, n, tiles, fill, more=True):
                V = n + 1
                pe.wait_ge(e["pair_done"], V)
                pe.wait_ge(e["n2_root"], V)
                pe.wait_ge(e["lw_in"], 48 * n + 48 if l == 0 else 64 * n - 64)
                pe.wait_ge(l_shift, 2 + 3 * l)
                pe.wait_ge(l_tanh, 2 + 2 * l)
                pe.wait_ge(l_ready, 1 + l)
                mm(mb[0][:, 0:SEQ], lw[0:64, 0, :], lact[0:64, 0, :], start=True, stop=True).then_inc(e["lora_w"], 1)
                mm(mb[1][:, 0:SEQ], lw[64:P, 0, :], lact[64:P, 0, :], start=True, stop=True).then_inc(e["lora_a"], 1)
                mm(mb[2][:, 0:SEQ], lw[:, 1, :], lact[:, 1, :], start=True, stop=True).then_inc(e["lora_g"], 1)
                if l:
                    mm(mb[3][:, 0:SEQ], lw[0:VRES, 2, :], lact[0:VRES, 2, :], start=True,
                       stop=True).then_inc(e["lora_v"], 1)
                fill(7)
                pe.wait_ge(e["t1_ready"], V)
                if l:
                    pe.wait_ge(e["v_tanh"], V - PAIRS)
                mm(mb[3][:, SEQ:2 * SEQ], blk, t1[:, :], start=True, stop=True).then_inc(e["bonus_sum"], 1)
                fill(4)
                pe.wait_ge(e["w_tanh"], V)
                pe.wait_ge(e["a_tanh"], V)
                if l:
                    pe.wait_ge(e["v_ready"], V - PAIRS)
                pe.wait_ge(e["scaled"], 4 * n + 4)
                for u in range(2):
                    for a, src in enumerate((btl[:, u, :], ktl[:, u, :], sh[:, 2, P * u:P * u + P])):
                        m = turned(mb[u][:, P * a:P * a + P], src, ident)
                    m.then_inc(e["turned"], 1)
                fill(2)
                for unit in range(4):
                    h, u = unit // 2, unit % 2
                    b = mb[(unit + 2) % 4]
                    if unit == 0:
                        pe.wait_ge(e["g_out"], V)
                    if unit == 1:
                        pe.wait_ge(e["bonus_ready"], V)
                    if unit >= 2:
                        pe.wait_ge(e["tm_ready"], 2 * n + unit - 1)
                    hs = slice(HEAD * h, HEAD * h + HEAD)
                    ar = AR[hs, u, :, :].rearrange("p a b -> p (a b)")
                    mm(b[:, 0:256], ktl[hs, u, :], ar, start=True, stop=True)
                    mm(b[:, 256:512], btl[hs, u, :], ar, start=True, stop=True).then_inc(e["gram_sum"], 1)
                    fill(1)
                pe.wait_ge(e["gram_ready"], 4 * n + 4)
                for unit in range(4):
                    m = turned(mb[2][:, P * unit:P * unit + P], G[:, unit, 2, :], ident)
                m.then_inc(e["n_turned"], 1)
                fill(1)
                for unit in range(4):
                    h, u = unit // 2, unit % 2
                    at = P * u + HEAD * h
                    m = mm(mb[3][:, at:at + HEAD], G[:, unit, 0, :], tm[:, u, 2, HEAD * h:HEAD * h + HEAD],
                           start=True, stop=True)
                m.then_inc(e["akv_sum"], 1)
                fill(1)
                for lv in range(1, LEVELS):
                    for w in range(2):
                        pe.wait_ge(e["level_done"], 2 * LEVELS * n + (2 if lv == 1 else 2 * lv - 1 + w))
                        if lv == 1 and w == 0:
                            pe.wait_ge(e["akv_out"], V)
                        for unit in (2 * w, 2 * w + 1):
                            at = HEAD * (unit % 2)
                            m = mm(packed(mb[2 + w][:, at:at + HEAD], lv), G[:, unit, 2, :],
                                   blocks(TT[:, unit, 0, :], lv, 0), start=True, stop=True)
                        m.then_inc(e["x_sum"], 1)
                    fill(1)
                    for w in range(2):
                        pe.wait_ge(e["x_out"], 2 * (LEVELS - 1) * n + 2 * lv - 1 + w)
                        for unit in (2 * w, 2 * w + 1):
                            at = HEAD * (unit % 2)
                            if lv < LEVELS - 1:
                                mm(packed(mb[w][:, at:at + HEAD], lv), TT[:, unit, 1, :],
                                   blocks(X[:, unit, :], lv, 0), start=True, stop=True)
                            m = mm(packed(mb[w][:, P + at:P + at + HEAD], lv), X[:, unit, :],
                                   blocks(TT[:, unit, 1, :], lv, 1), start=True, stop=True)
                        m.then_inc(e["t_sum"], 1)
                    fill(1)
                wait_alone(pe, e["level_done"], 2 * LEVELS * (n + 1))
                for c in range(NCH):
                    u, rows = c // 2, slice(CHUNK * (c % 2), CHUNK * (c % 2) + CHUNK)
                    if c:
                        pe.wait_ge(e["s_out"], (NCH - 1) * n + c)
                        mm(mb[0][rows, 0:P], AR[:, u, 0, rows], St[:, c, :], start=True,
                           stop=True).then_inc(e["r_sum"], 1)
                        fill(1)
                        wait_alone(pe, e["r_out"], (NCH - 1) * n + c)
                    rhs = Rb if c else AKV
                    for h in range(2):
                        hs = slice(HEAD * h, HEAD * h + HEAD)
                        m = mm(mb[0][rows, P + HEAD * h:P + HEAD * h + HEAD], TT[rows, 2 * h + u, 1, rows],
                               rhs[rows, u, hs], start=True, stop=True)
                    m.then_inc(e["u_sum"], 1)
                    m = mm(mb[3][rows, P * u:P * u + P], AR[:, u, 1, rows], St[:, c, :], start=True, stop=False,
                           skip_group_check=True)
                    if c == 0:
                        m.then_inc(e["x_free"], 1)
                    if c < NCH - 1:
                        mm(mb[2][:, 0:P], tm[rows, u, 1, :], tm[rows, u, 2, :], start=True, stop=False)
                    fill(1)
                    pe.wait_ge(e["u_out"], NCH * n + c + 1)
                    if c < NCH - 1:
                        mm(mb[2][:, 0:P], tm[rows, u, 0, :], U[rows, u, :], start=False,
                           stop=True).then_inc(e["s_sum"], 1)
                    if c % 2:
                        for h in range(2):
                            hs = slice(HEAD * h, HEAD * h + HEAD)
                            at = P * u + HEAD * h
                            mm(mb[3][:, at:at + HEAD], G[:, 2 * h + u, 1, :], tm[:, u, 2, hs], start=False,
                               stop=False, skip_group_check=True)
                            m = mm(mb[3][:, at:at + HEAD], G[:, 2 * h + u, 3, :], U[:, u, hs], start=False,
                                   stop=True, skip_group_check=True)
                        m.then_inc(e["y_sum"], 1)
                    if c == 0:
                        pe.wait_ge(e["roped"], V)
                        mm(mb[1][:, 0:P], qr[:, 0, 0:P], qr[:, 1, 0:P], start=True, stop=True)
                        mm(mb[1][:, P:3 * P], qr[:, 0, P:2 * P], qr[:, 1, :], start=True,
                           stop=True).then_inc(e["score_sum"], 1)
                    elif c < NCH - 1:
                        fill(1)
                pe.wait_ge(e["masked"], V)
                for u in range(2):
                    m = turned(mb[1][:, P * u:P * u + P], zt[:, 5, 1 + P * u:1 + P * u + P], ident)
                m.then_inc(e["va_turned"], 1)
                if more:
                    key_norms(n + 1)
                pe.wait_ge(e["probs"], V)
                for j in range(3):
                    m = turned(mb[2][:, P * j:P * j + P], sm[:, P * j:P * j + P], ident)
                m.then_inc(e["p_turned"], 1)
                fill(2)
                pe.wait_ge(e["va_out"], V)
                pe.wait_ge(e["p_out"], V)
                mm(mb[1][:, 0:2 * P], vt[:, 0, :], pt[:, 0:2 * P], start=True, stop=False)
                mm(mb[1][:, P:2 * P], vt[:, 1, :], pt[:, 2 * P:3 * P], start=False, stop=True).then_inc(e["o_sum"], 1)
                fill(2)
                if more:
                    pe.wait_ge(e["n2_root"], V + 1)
                pe.wait_ge(e["y_norm"], V)
                for u in range(2):
                    m = turned(mb[0][:, P * u:P * u + P], yn[:, u, :], ident)
                m.then_inc(e["y_turned"], 1)
                fill(48)

            for l in range(DEPTH):
                if l == 0:
                    x_sum(0)
                k, t = start[l, "lora"]
                group(k, 0, t, hT, 2 * (1 - l), lambda kt: tile_made(2 * l, kt))
                if l == 0:
                    pe.wait_ge(prm_in, 16 * (8 + 8 + 2))
                    for j in range(2):
                        m = turned(mb[2][:, P * j:P * j + P], stage[:, j, :], ident)
                    m.then_inc(prm_turned, 1)
                if l:
                    k, t = start[l, "vres"]
                    r = k % ROUND
                    pe.wait_ge(tile_out, t)
                    pe.wait_ge(hi_done, k + 1)
                    pe.wait_ge(lo_done, k + 1)
                    for kt in range(KT):
                        cols = slice(VRES * kt, VRES * kt + P)
                        pair = hT[:, kt, :, :].rearrange("p a b -> p (a b)")
                        if kt == 0:
                            mm(bank[2][:, :], whi[r][:, cols], pair, start=True, stop=False)
                        m = mm(bank[2][:, 0:SEQ], wlo[r][:, cols], hT[:, kt, 0, :], start=False, stop=False)
                        if kt:
                            m = mm(bank[2][:, :], whi[r][:, cols], pair, start=False, stop=kt == KT - 1)
                    m.then_inc(slot_used, 1)
                k, t = start[l, "pairs"]
                group(k, 0, l and t - 1, hT, 0)
                group(k + 4, 0, t, hT, 2)

                def filler(ticks, end):
                    at = [0]

                    def fill(m):
                        ticks(at[0], min(end, at[0] + m))
                        at[0] = min(end, at[0] + m)
                    return fill
                if l:
                    pe.wait_ge(e["pair_done"], PAIRS + 1)
                pe.wait_ge(inv_x, 2 * l + 1)
                key_norms(PAIRS * l)
                loop(pe, PAIRS - 1, lambda i: mixer(l, i, PAIRS * l + i, t + 4 + i * 6, filler(
                    lambda a, b: pair_ticks(a, b, k + 8, i * 3, t + 4 + i * 6), 48)))
                mixer(l, PAIRS - 1, PAIRS * l + PAIRS - 1, t + 46, filler(
                    lambda a, b: last_ticks(a, b, k + 92, t + 46), 40), False)
                pe.wait_ge(e["o_lo"], PAIRS * (l + 1))
                for order in ((2, 3, 0), (1,)):
                    if order == (1,):
                        pe.wait_ge(e["pair_done"], PAIRS * (l + 1) + 1)
                    for g in range(2):
                        for j in order:
                            tick(k + 102 + g, 0, j, mT, OUT_TILES[3][j], 2 * g, False, j == 1, 2, 1)
                k, t = start[l, "out"]

                def turn(i):
                    for g in range(2):
                        group(k + 8 + 4 * g, i * 2, t + 2 + 2 * g + i * 4, mT, 2 * g)
                loop(pe, 3, turn)
                y_sum(2 * l)
                pe.wait_ge(root_y, 2 * l + 1)
                x_sum(2 * l + 1)
                k, t = start[l, "mlp"]
                for q0, nq, last in runs(l):
                    def quarter(q):
                        qq = q + q0

                        def up_turn(i):
                            for g in range(2):
                                group(k + 4 * g, qq * 16 + i * 2, t + 2 * g - 2 + qq * 32 + i * 4, hT, 2 * g,
                                      lambda kt: None if g else tile_made(2 * l + 1, kt))
                        loop(pe, 4, up_turn)
                        def down_turn(i):
                            for g in range(2):
                                group(k + 32 + 4 * g, qq * 16 + i * 2, t + 16 + 2 * g - 2 + qq * 32 + i * 4, mT,
                                      2 * g, lambda kt: (tile_out, t + 16 + qq * 32) if kt == 14 and not g else None)
                        loop(pe, 4, down_turn)
                    loop(pe, nq, quarter)
                y_sum(2 * l + 1)
                if l < DEPTH - 1:
                    pe.wait_ge(root_y, 2 * l + 2)
                    x_sum(2 * l + 2)
            for q in range(4):
                for who in range(2):
                    pe.wait_ge(step_y[who], taken(2 * DEPTH - 1, 4 * q + 3, who))
                if q == 2:
                    pe.wait_ge(root_y, 2 * DEPTH)
                for u in range(2):
                    for j in range(4):
                        m = turned((bank + mb)[2 * q + u][:, P * j:P * j + P], xT[:, 4 * q + j, P * u:P * u + P],
                                   ident)
                    m.then_inc(out_turned, 1)

        @block.scalar
        def _(act):
            f = nc.scalar.activation

            def hi(k, d=0):
                if isinstance(d, int) and k + 4 * d >= N_SLOTS:
                    return
                r = k % ROUND
                act.wait_ge(landed[r], 32 * (k // ROUND + 1) + 32 * d)
                if not (isinstance(d, int) and k + 4 * d < ROUND):
                    act.wait_ge(slot_used, k + 4 * d - ROUND + 1)
                f(whi[r][:, :], raw[r][:, :, :].rearrange("p a b -> p (a b)"), ACT.Copy).then_inc(hi_done, 1)

            def halves(k, d, tiles, b0, n=2):
                act.wait_ge(slot_used, k + 4 * d + 1)
                if not (isinstance(tiles, int) and tiles <= 0):
                    act.wait_ge(tile_out, tiles)
                for b in range(n):
                    f(xl[:, b, :], bank[b0 + b][:, SEQ:2 * SEQ], ACT.Copy).then_inc(half_out, 1)

            def group(k, d, tiles, b0):
                for j in range(4):
                    hi(k + LEAD + j, d)
                halves(k + 3, d, tiles, b0)

            def x_squares(m, waits, between={}):
                for j in range(KT):
                    for semaphore, value in waits(j):
                        act.wait_ge(semaphore, value)
                    if KT * m + j >= 3:
                        act.wait_ge(used_x, KT * m + j - 2)
                    f(sh[:, j % 3, :], xT[:, j, :], ACT.Square).then_inc(sq_x, 1)
                    if j in between:
                        hi(between[j])

            def y_squares(m, a, i, t):
                act.wait_ge(tile_out, t)
                if m:
                    act.wait_ge(sum_y, m)
                for b in range(2):
                    if m or a + b >= 4:
                        act.wait_ge(used_y, Y_SUMMED * m + a + b - 3 + i * 4)
                    f(zt[:, (a + b) % 4, 1:], yo[:, bass.ds(i * 4 + a + b, 1), :].rearrange("p a b -> p (a b)"),
                      ACT.Square).then_inc(sq_y, 1)

            def x_norm(m):
                act.wait_ge(used_x, KT * (m + 1))
                f(t1[:, :], mb[0][:, 0:SEQ], ACT.Sqrt, bias=col_eps, scale=1.0 / D).then_inc(root_x, 1)
                for j in range(KT):
                    act.wait_ge(h_f, KT * m + j + 1)
                    f(hT[:, j, 0, :], yo[:, j, :], ACT.Copy).then_inc(h_hi, 1)

            def y_root(m):
                act.wait_ge(sum_y, m + 1)
                f(rn[:, :], mb[0][:, 0:SEQ], ACT.Sqrt, bias=col_eps, scale=1.0 / D).then_inc(root_y, 1)
                if m < 2 * DEPTH - 1:
                    x_squares(m + 1, lambda j: [(step_y[int(j in POOL_TILES)], taken(m, j, int(j in POOL_TILES)))])

            def key_norms(n):
                act.wait_ge(e["n2_sum"], n + 1)
                f(rn[:, :], mb[0][:, SEQ:2 * SEQ], ACT.Sqrt).then_inc(e["n2_root"], 1)

            def mixer(l, i, n, tiles, step, finish, more=True):
                V = n + 1
                half = lambda c: drv[:, l, bass.ds(c + i, 1)]
                step(-1)
                finish(-1)
                act.wait_ge(e["lora_w"], V)
                f(eN[:, :, :].rearrange("p a b -> p (a b)"), mb[0][:, 0:SEQ], ACT.Tanh, bias=half(HALF),
                  scale=0.5).then_inc(e["w_tanh"], 1)
                act.wait_ge(e["lora_a"], V)
                f(ta[:, :], mb[1][:, 0:SEQ], ACT.Tanh, bias=half(HALF + 8), scale=0.5).then_inc(e["a_tanh"], 1)
                if l:
                    act.wait_ge(e["lora_v"], V - PAIRS)
                    f(xs[:, 0, :], mb[3][:, 0:SEQ], ACT.Tanh, bias=half(HALF + 16), scale=0.5).then_inc(e["v_tanh"], 1)
                act.wait_ge(e["cum_ready"], V)
                f(eP[:, :, :], cs[:, :, :], ACT.Exp, bias=col_shift).then_inc(e["e_pos"], 1)
                f(eN[:, :, :], cs[:, :, 1:], ACT.Exp, bias=col_nshift, scale=-1.0).then_inc(e["e_neg"], 1)
                f(eC[:, :], cs[:, :, CHUNK], ACT.Exp).then_inc(e["e_chunk"], 1)
                step(0)
                act.wait_ge(e["lora_g"], V)
                f(gs[:, :], mb[2][:, 0:SEQ], ACT.Copy).then_inc(e["g_out"], 1)
                step(1)
                for u in range(2):
                    act.wait_ge(e["turned"], 2 * n + u + 1)
                    f(tm[:, u, :, :].rearrange("p a b -> p (a b)"), mb[u][:, 0:384], ACT.Copy)\
                        .then_inc(e["tm_ready"], 1)
                step(2)
                step(3)
                act.wait_ge(e["akv_sum"], V)
                f(AKV[:, :, :].rearrange("p a b -> p (a b)"), mb[3][:, 0:256], ACT.Copy).then_inc(e["akv_out"], 1)
                for lv in range(1, LEVELS):
                    for w in range(2):
                        act.wait_ge(e["x_sum"], 2 * (LEVELS - 1) * n + 2 * lv - 1 + w)
                        f(blocks(X[:, 2 * w:2 * w + 2, :], lv, 0),
                          packed(mb[2 + w][:, 0:P].rearrange("p (a b) -> p a b", a=2), lv),
                          ACT.Copy).then_inc(e["x_out"], 1)
                    if lv == 1:
                        finish(0)
                        step(4)
                    if lv == 2:
                        act.wait_ge(tile_out, tiles + 2)
                        for a, b in ((0, 64), (64, 0)):
                            f(xs[a:a + 64, :, :], zt[b:b + 64, 3:5, 1:SEQ + 1], ACT.Copy).then_inc(e["swapped"], 1)
                    if lv == 3:
                        step(5)
                    if lv == 4:
                        step(6)
                for c in range(NCH):
                    u, rows = c // 2, slice(CHUNK * (c % 2), CHUNK * (c % 2) + CHUNK)
                    act.wait_ge(e["u_sum"], NCH * n + c + 1)
                    f(U[rows, u, :], mb[0][rows, P:2 * P], ACT.Copy).then_inc(e["u_out"], 1)
                    if c == 0:
                        step(7)
                    if c == 2:
                        finish(1)
                    if c == 3:
                        act.wait_ge(e["nmax"], V)
                        for a, (x0, x1) in enumerate(((0, P), (P, 3 * P))):
                            f(sm[:, x0:x1], sm[:, x0:x1], ACT.Exp, bias=small[:, 10 + a:11 + a], scale=SCALE,
                              accum_out=small[:, 12 + a:13 + a]).then_inc(e["expd"], 1)
                        f(spare[:, :], col_eps, ACT.Sqrt)
                act.wait_ge(e["va_turned"], V)
                f(vt[:, :, :].rearrange("p a b -> p (a b)"), mb[1][:, 0:256], ACT.Copy).then_inc(e["va_out"], 1)
                act.wait_ge(e["p_turned"], V)
                f(pt, mb[2][:, 0:384], ACT.Copy).then_inc(e["p_out"], 1)
                act.wait_ge(e["y_cen"], V)
                f(ysq[:, :, :], yn[:, :, :], ACT.Square).then_inc(e["y_sq"], 1)
                act.wait_ge(e["y_var"], V)
                f(small[:, 4:8], small[:, 4:8], ACT.Sqrt, bias=col_lnx, scale=1.0 / HEAD).then_inc(e["y_root"], 1)
                if more:
                    key_norms(n + 1)
                def attention_hi():
                    act.wait_ge(e["o_sum"], V)
                    f(mT[:, bass.ds(PAIRS + i, 1), 0, :], mb[1][:, 0:256].unsqueeze(1),
                      ACT.Copy).then_inc(e["o_hi"], 1)
                if not more:
                    attention_hi()
                step(8)
                step(9)
                if more:
                    attention_hi()
                step(10)
                act.wait_ge(e["y_gated"], V)
                f(mT[:, bass.ds(i, 1), 0, :], yf[:, :].unsqueeze(1), ACT.Copy).then_inc(e["y_hi"], 1)

            act.wait_ge(first_in, 16)
            x_squares(0, lambda j: [(x_ready, j // 2 + 1)], {7: 0, 11: 1, 15: 2})
            for l in range(DEPTH):
                x_norm(2 * l)
                k, t = start[l, "lora"]
                group(k, 0, t, 2 * (1 - l))
                if l:
                    k, t = start[l, "vres"]
                    hi(k + LEAD)
                    halves(k, 0, t, 2, 1)
                act.wait_ge(l_shift, 1 + 2 * l)
                f(lact[0:64, 0, :], lact[0:64, 0, :], ACT.Tanh).then_inc(l_tanh, 1)
                act.wait_ge(l_shift, 2 + 2 * l)
                f(lact[:, 1, :], lact[:, 1, :], ACT.Tanh, scale=0.5).then_inc(l_tanh, 1)
                k, t = start[l, "pairs"]
                group(k, 0, t, 0)
                for j in range(3):
                    hi(k + 4 + LEAD + j)

                def turn(i):
                    def finish(g):
                        halves(k + 11 + 4 * g, i * 3, t + 4 + 2 * g + i * 6, (2, 2, 0)[g + 1])
                    mixer(l, i, PAIRS * l + i, t + 4 + i * 6, lambda j: hi(k + 8 + j + LEAD, i * 3), finish)
                key_norms(PAIRS * l)
                loop(act, PAIRS - 1, turn)

                def finish(g):
                    if g < 1:
                        halves(k + 95 + 4 * g, 0, t + 46 + 2 * g, 2)
                mixer(l, PAIRS - 1, PAIRS * l + PAIRS - 1, t + 46,
                      lambda j: hi(k + 92 + j + LEAD) if j < 10 else None, finish, False)
                k, t = start[l, "out"]
                for g in range(2):
                    hi(k + 6 + g + LEAD)
                    halves(k + 6 + g, 0, t + 2 * g, 2 * g)
                    act.wait_ge(e["pair_done"], PAIRS * (l + 1) + 1)
                    y_squares(2 * l, 2 * g, 0, t + 2 * g + 2)

                def turn(i):
                    for g in range(2):
                        group(k + 8 + 4 * g, i * 2, t + 4 + 2 * g + i * 4, 2 * g)
                        y_squares(2 * l, 4 + 2 * g, i, t + 6 + 2 * g + i * 4)
                loop(act, 3, turn)
                y_root(2 * l)
                x_norm(2 * l + 1)
                k, t = start[l, "mlp"]
                for q0, nq, last in runs(l):
                    def quarter(q):
                        qq = q + q0

                        def up_turn(i):
                            for g in range(2):
                                T = t + 2 * g + qq * 32 + i * 4
                                group(k + 4 * g, qq * 16 + i * 2, T, 2 * g)
                                for b in range(2):
                                    act.wait_ge(up_relu, 64 * l + 2 * g + b + 1 + qq * 16 + i * 4)
                                    f(mT[:, bass.ds(i * 4 + 2 * g + b, 1), 0, :],
                                      AR[:, b, :, :].rearrange("p a b -> p (a b)").unsqueeze(1),
                                      ACT.Copy).then_inc(up_hi, 1)
                        loop(act, 4, up_turn)

                        def down_turn(i):
                            for g in range(2):
                                group(k + 32 + 4 * g, qq * 16 + i * 2, t + 16 + 2 * g + qq * 32 + i * 4, 2 * g)
                                if last:
                                    y_squares(2 * l + 1, 2 * g, i, t + 18 + 2 * g + qq * 32 + i * 4)
                        loop(act, 3 if last else 4, down_turn)
                        if last:
                            down_turn(3)
                    loop(act, nq, quarter)
                y_root(2 * l + 1)
            act.wait_ge(lo_done, N_SLOTS)
            for q in range(4):
                for u in range(2):
                    act.wait_ge(out_turned, 2 * q + u + 1)
                    f(raw[q][:, 2 * u:2 * u + 2, :].rearrange("p a b -> p (a b)"), (bank + mb)[2 * q + u][:, :],
                      ACT.Copy).then_inc(out_copied, 1)

        @block.vector
        def _(dve):
            tt, ts, stt = nc.vector.tensor_tensor, nc.vector.tensor_scalar, nc.vector.scalar_tensor_tensor
            flat = lambda ap: ap.rearrange("p a b -> p (a b)")

            def lo(k, d=0):
                if isinstance(d, int) and k + 4 * d >= N_SLOTS:
                    return
                r = k % ROUND
                dve.wait_ge(hi_done, k + 4 * d + 1)
                tt(wlo[r][:, :], flat(raw[r][:, :, :]), whi[r][:, :].bitcast(F32), ALU.subtract).then_inc(lo_done, 1)

            def sums(tiles, b0, dest, n=2):
                for b in range(n):
                    dve.wait_ge(half_out, tiles + b + 1)
                    tt(dest(b), bank[b0 + b][:, 0:SEQ], xl[:, b, :], ALU.add).then_inc(tile_out, 1)

            def splits(k, d):
                for j in range(4):
                    lo(k + LEAD + j, d)

            def x_norm(m, l, gain):
                dve.wait_ge(root_x, m + 1)
                nc.vector.reciprocal(t1[:, :], t1[:, :]).then_inc(inv_x, 1)
                dve.wait_ge(inv_x, m + 1)

                def rest(j):
                    if j not in POOL_LO:
                        dve.wait_ge(h_hi, KT * m + j + 1)
                        tt(hT[:, j, 1, :], yo[:, j, :], hT[:, j, 0, :].bitcast(F32),
                           ALU.subtract).then_inc(h_ready[0], 1)
                for j in range(KT):
                    stt(yo[:, j, :], xT[:, j, :], gain(j), t1[:, :], ALU.mult, ALU.mult).then_inc(h_f, 1)
                    if j >= 2:
                        rest(j - 2)
                rest(KT - 2)
                rest(KT - 1)

            def y_norm(m, gain):
                dve.wait_ge(root_y, m + 1)
                nc.vector.reciprocal(rn[:, :], rn[:, :]).then_inc(inv_y, 1)
                dve.wait_ge(inv_y, m + 1)

                def add(j):
                    if j not in POOL_TILES:
                        dve.wait_ge(scaled_y, KT * m + j + 1)
                        tt(xT[:, j, :], xT[:, j, :], yo[:, j, :], ALU.add).then_inc(step_y[0], 1)
                for j in range(KT):
                    stt(yo[:, j, :], yo[:, j, :], gain(j), rn[:, :], ALU.mult, ALU.mult).then_inc(scaled_y, 1)
                    if j:
                        add(j - 1)
                add(KT - 1)
                for who in range(2):
                    dve.wait_ge(step_y[who], taken(m, KT - 1, who))

            def gain(l, which):
                return lambda j: prm[:, 2, 32 * which + 16 * l + j:32 * which + 16 * l + j + 1]

            def key_norms(l, i, n):
                col = lambda c: prm[:, l, bass.ds(c + i, 1)]
                for m, j in enumerate((1, 0)):
                    dve.wait_ge(e["diffed"], 3 * n + m + 1)
                    stt(sh[:, j, :], dsh[:, j, :], col(MU + PAIRS * j), zt[:, j, 1:], ALU.mult,
                        ALU.add).then_inc(e["shifted"], 1)
                dve.wait_ge(e["shifted"], 3 * n + 1)
                stt(rn[:, :], sh[:, 1, :], drv[:, l, bass.ds(KK2 + i, 1)], sh[:, 1, :], ALU.mult,
                    ALU.mult).then_inc(e["kk_sq"], 1)

            def mixer(l, i, n, tiles, step, finish, more=True):
                V = n + 1
                col = lambda c: prm[:, l, bass.ds(c + i, 1)]
                der = lambda c: drv[:, l, bass.ds(c + i, 1)]
                finish(-1)
                dve.wait_ge(e["n2_root"], V)
                ts(rn[:, :], rn[:, :], 1e-12, None, ALU.max).then_inc(e["n2_max"], 1)
                dve.wait_ge(e["n2_max"], V)
                nc.vector.reciprocal(rn[:, :], rn[:, :]).then_inc(e["n2_inv"], 1)
                dve.wait_ge(e["w_tanh"], V)
                ts(ldc[:, :, 1:], eN[:, :, :], -DECAY_C, -DECAY_C, ALU.mult, ALU.add).then_inc(e["ld_ready"], 1)
                dve.wait_ge(e["ld_ready"], V)
                nc.vector.tensor_tensor_scan(flat(cs[:, :, :]), hp, flat(ldc[:, :, :]), 0.0, ALU.mult,
                                             ALU.add).then_inc(e["cum_ready"], 1)
                dve.wait_ge(e["a_tanh"], V)
                ts(kf[:, :], ta[:, :], der(HKA), der(OMKA), ALU.mult, ALU.add).then_inc(e["kf_ready"], 1)
                ts(ta[:, :], ta[:, :], -0.5, -0.5, ALU.mult, ALU.add).then_inc(e["af_ready"], 1)
                dve.wait_ge(e["kf_ready"], V)
                tt(kf[:, :], sh[:, 1, :], kf[:, :], ALU.mult).then_inc(e["k2_ready"], 1)
                dve.wait_ge(e["k2_ready"], V)
                stt(t1[:, :], sh[:, 0, :], col(RK), kf[:, :], ALU.mult, ALU.mult).then_inc(e["t1_ready"], 1)
                dve.wait_ge(tile_out, tiles)
                dve.wait_ge(e["diffed"], 3 * n + 3)
                stt(sh[:, 2, :], dsh[:, 2, :], col(MU + PAIRS * 2), zt[:, 2, 1:], ALU.mult,
                    ALU.add).then_inc(e["shifted"], 1)
                if l:
                    dve.wait_ge(e["v_tanh"], V - PAIRS)
                    ts(xs[:, 0, :], xs[:, 0, :], 0.5, 0.5, ALU.mult, ALU.add).then_inc(e["v_gate"], 1)
                dve.wait_ge(e["n2_inv"], V)
                stt(rn[:, :], sh[:, 1, :], der(NKK), rn[:, :], ALU.mult, ALU.mult).then_inc(e["kk_ready"], 1)
                dve.wait_ge(e["kk_ready"], V)
                dve.wait_ge(e["af_ready"], V)
                tt(ta[:, :], rn[:, :], ta[:, :], ALU.mult).then_inc(e["b_ready"], 1)
                dve.wait_ge(e["e_pos"], V)
                cc = lambda ap: ap.rearrange("p (c t) -> p c t", t=CHUNK)
                for u in range(2):
                    c4 = slice(2 * u, 2 * u + 2)
                    toks = slice(P * u, P * u + P)
                    tt(cc(AR[:, u, 0, :]), cc(rn[:, toks]), eP[:, c4, 0:CHUNK], ALU.mult)
                    tt(cc(AR[:, u, 1, :]), cc(sh[:, 0, toks]), eP[:, c4, 1:], ALU.mult).then_inc(e["scaled"], 1)
                dve.wait_ge(e["e_neg"], V)
                tt(flat(ktl[:, :, :]), kf[:, :], flat(eN[:, :, :]), ALU.mult).then_inc(e["scaled"], 1)
                dve.wait_ge(e["b_ready"], V)
                tt(flat(btl[:, :, :]), ta[:, :], flat(eN[:, :, :]), ALU.mult).then_inc(e["scaled"], 1)
                step(0)
                step(1)
                dve.wait_ge(e["bonus_sum"], V)
                if l:
                    dve.wait_ge(e["v_ready"], V - PAIRS)
                tt(t1[:, :], mb[3][:, SEQ:2 * SEQ], sh[:, 2, :], ALU.mult).then_inc(e["bonus_ready"], 1)
                step(2)
                for unit in range(4):
                    dve.wait_ge(e["gram_sum"], 4 * n + unit + 1)
                    tt(G[:, unit, :, :].rearrange("p a b -> p (a b)"), mb[(unit + 2) % 4][:, :],
                       cst[:, C_GRAM:C_GRAM + 512], ALU.mult).then_inc(e["gram_ready"], 1)
                wait_alone(dve, e["tt_reset"], 8 * n + 8)
                wait_alone(dve, e["n_turned"], V)
                wait_alone(dve, e["gram_ready"], 4 * n + 4)
                mask = lambda lv, j: packed(lvl[:, lv, j, :].unsqueeze(1).to_broadcast([P, 2, HEAD]), lv)
                for w in range(2):
                    us = slice(2 * w, 2 * w + 2)
                    n_t = mb[2][:, 256 * w:256 * w + 256].rearrange("p (a b) -> p a b", a=2)
                    nc.vector.copy_predicated(blocks(TT[:, us, 0, :], 0, 0), mask(0, 0), blocks(n_t, 0, 0))
                    nc.vector.copy_predicated(blocks(TT[:, us, 1, :], 0, 1), mask(0, 1),
                                              blocks(G[:, us, 2, :], 0, 1)).then_inc(e["level_done"], 1)
                step(3)
                for lv in range(1, LEVELS):
                    for w in range(2):
                        us = slice(2 * w, 2 * w + 2)
                        wait_alone(dve, e["t_sum"], 2 * (LEVELS - 1) * n + 2 * lv - 1 + w)
                        new = lambda j: packed(mb[w][:, P * j:P * j + P].rearrange("p (a b) -> p a b", a=2), lv)
                        if lv < LEVELS - 1:
                            nc.vector.copy_predicated(blocks(TT[:, us, 0, :], lv, 0), mask(lv, 0), new(0))
                        nc.vector.copy_predicated(blocks(TT[:, us, 1, :], lv, 1), mask(lv, 1),
                                                  new(1)).then_inc(e["level_done"], 1)
                    if lv == 1:
                        finish(0)
                        step(4)
                    if lv == 2:
                        dve.wait_ge(tile_out, tiles + 2)
                        tt(qr[:, :, :], zt[:, 3:5, 1:],
                           cst[:, C_COS:C_COS + SEQ].unsqueeze(1).to_broadcast([P, 2, SEQ]),
                           ALU.mult).then_inc(e["roped_c"], 1)
                    if lv == 2:
                        dve.wait_ge(e["g_out"], V)
                        dve.wait_ge(e["bonus_ready"], V)
                        stt(t1[:, :], t1[:, :], col(LB), gs[:, :], ALU.add, ALU.mult).then_inc(e["y_bonus"], 1)
                        dve.wait_ge(e["y_bonus"], V)
                        ts(gs[:, :], gs[:, :], col(LG), None, ALU.mult).then_inc(e["y_gain"], 1)
                    if lv == 3:
                        dve.wait_ge(e["swapped"], 2 * n + 2)
                        tt(xs[:, :, :], xs[:, :, :],
                           cst[:, C_SIN:C_SIN + SEQ].unsqueeze(1).to_broadcast([P, 2, SEQ]),
                           ALU.mult).then_inc(e["roped_s"], 1)
                        step(5)
                    if lv == 4:
                        step(6)
                        dve.wait_ge(e["roped_c"], V)
                        dve.wait_ge(e["roped_s"], V)
                        tt(qr[:, :, :], qr[:, :, :], xs[:, :, :], ALU.add).then_inc(e["roped"], 1)
                dve.wait_ge(e["akv_out"], V)
                dve.wait_ge(e["e_chunk"], V)
                for c in range(NCH):
                    u, rows = c // 2, slice(CHUNK * (c % 2), CHUNK * (c % 2) + CHUNK)
                    if c:
                        dve.wait_ge(e["r_sum"], (NCH - 1) * n + c)
                        tt(Rb[rows, u, :], mb[0][rows, 0:P], AKV[rows, u, :], ALU.add).then_inc(e["r_out"], 1)
                    if c == 1:
                        step(7)
                        dve.wait_ge(e["score_sum"], V)
                        tt(sm[:, :], mb[1][:, 0:384], cst[:, C_CAUS:C_CAUS + 384], ALU.add).then_inc(e["masked"], 1)
                        dve.wait_ge(e["masked"], V)
                        nc.vector.tensor_reduce(small[:, 8:9], sm[:, 0:P], AX.X, ALU.max)
                        nc.vector.tensor_reduce(small[:, 9:10], sm[:, P:3 * P], AX.X, ALU.max).then_inc(e["smax"], 1)
                    if c == 2:
                        dve.wait_ge(e["smax"], V)
                        ts(small[:, 10:12], small[:, 8:10], -SCALE, None, ALU.mult).then_inc(e["nmax"], 1)
                        finish(1)
                    if c < NCH - 1:
                        dve.wait_ge(e["s_sum"], (NCH - 1) * n + c + 1)
                        stt(Stmp, mb[2][:, 0:P], eC[:, c:c + 1], blk, ALU.mult,
                            ALU.mult).then_inc(e["s_tmp"], 1)
                        dve.wait_ge(e["s_tmp"], (NCH - 1) * n + c + 1)
                        stt(St[:, c + 1, :], St[:, c, :], eC[:, c:c + 1], Stmp, ALU.mult,
                            ALU.add).then_inc(e["s_out"], 1)
                        if c < NCH - 2:
                            dve.wait_ge(e["s_out"], (NCH - 1) * n + c + 1)
                if more:
                    key_norms(l, i + 1, n + 1)
                dve.wait_ge(e["expd"], 2 * n + 2)
                nc.vector.reciprocal(small[:, 14:16], small[:, 12:14]).then_inc(e["rsum"], 1)
                dve.wait_ge(e["rsum"], V)
                ts(sm[:, 0:P], sm[:, 0:P], small[:, 14:15], None, ALU.mult)
                ts(sm[:, P:3 * P], sm[:, P:3 * P], small[:, 15:16], None, ALU.mult).then_inc(e["probs"], 1)
                ys = mb[3][:, 0:256].rearrange("p (a b) -> p a b", b=HEAD)
                y4 = flat(yn[:, :, :]).rearrange("p (a b) -> p a b", b=HEAD)
                wide = lambda ap: ap.unsqueeze(2).to_broadcast([P, 4, HEAD])
                dve.wait_ge(e["y_sum"], 2 * n + 2)
                nc.vector.tensor_reduce(small[:, 0:4], ys, AX.X, ALU.add).then_inc(e["y_mean"], 1)
                dve.wait_ge(e["y_mean"], 2 * n + 1)
                ts(small[:, 0:4], small[:, 0:4], 1.0 / HEAD, None, ALU.mult).then_inc(e["y_mean"], 1)
                dve.wait_ge(e["y_mean"], 2 * n + 2)
                tt(y4, ys, wide(small[:, 0:4]), ALU.subtract).then_inc(e["y_cen"], 1)
                dve.wait_ge(e["y_sq"], V)
                nc.vector.tensor_reduce(small[:, 4:8], flat(ysq[:, :, :]).rearrange("p (a b) -> p a b", b=HEAD),
                                        AX.X, ALU.add).then_inc(e["y_var"], 1)
                dve.wait_ge(e["y_root"], V)
                nc.vector.reciprocal(small[:, 4:8], small[:, 4:8]).then_inc(e["y_rinv"], 1)
                dve.wait_ge(e["y_rinv"], V)
                tt(y4, y4, wide(small[:, 4:8]), ALU.mult).then_inc(e["y_norm"], 1)

                def attention_lo():
                    dve.wait_ge(e["o_hi"], V)
                    tt(mT[:, bass.ds(PAIRS + i, 1), 1, :], mb[1][:, 0:256].unsqueeze(1),
                       mT[:, bass.ds(PAIRS + i, 1), 0, :].bitcast(F32), ALU.subtract).then_inc(e["o_lo"], 1)
                if not more:
                    attention_lo()
                step(8)
                dve.wait_ge(e["y_turned"], V)
                dve.wait_ge(e["y_gain"], V)
                tt(yf[:, :], mb[0][:, 0:SEQ], gs[:, :], ALU.mult).then_inc(e["y_scaled"], 1)
                dve.wait_ge(e["y_scaled"], V)
                tt(yf[:, :], yf[:, :], t1[:, :], ALU.add).then_inc(e["y_gated"], 1)
                if more:
                    attention_lo()
                if l == 0:
                    dve.wait_ge(e["v_kept"], V)
                dve.wait_ge(e["y_hi"], V)
                tt(mT[:, bass.ds(i, 1), 1, :], yf[:, :].unsqueeze(1), mT[:, bass.ds(i, 1), 0, :].bitcast(F32),
                   ALU.subtract).then_inc(e["pair_done"], 1)
                step(9)

            for b8 in range(8):
                dve.wait_ge(x_turned, b8 + 1)
                nc.vector.tensor_copy(flat(xT[:, 2 * b8:2 * b8 + 2, :]), (bank + mb)[b8][:, :]).then_inc(x_ready, 1)
            dve.wait_ge(gain_turned, 1)
            nc.vector.tensor_copy(prm[:, 2, :], mb[1][:, 0:P]).then_inc(gain_ready, 1)
            dve.wait_ge(x_ready, 8)
            dve.wait_ge(gain_ready, 1)
            for j in range(LEAD):
                lo(j)

            def parameters():
                dve.wait_ge(const_in, 48)
                for place, a, b in ((qr, 0, 4), (xs, 4, LEVELS)):
                    nc.vector.tensor_copy(lvl[:, a:b, :, :].rearrange("p a b c -> p (a b c)"),
                                          flat(place[:, :, :])[:, 0:P * (b - a)]).then_inc(lvl_ready, 1)
                dve.wait_ge(lvl_ready, 2)
                dve.wait_ge(prm_turned, 1)
                nc.vector.tensor_copy(flat(prm[:, 0:2, :]), mb[2][:, 0:256]).then_inc(prm_ready, 1)
                dve.wait_ge(prm_ready, 1)
                for l in range(DEPTH):
                    pl = lambda c, n=8: prm[:, l, c:c + n]
                    ts(drv[:, l, HALF:HALF + 24], pl(W0, 24), 0.5, None, ALU.mult)
                    ts(drv[:, l, HKA:HKA + 8], pl(KA), 0.5, None, ALU.mult)
                    ts(drv[:, l, OMKA:OMKA + 8], pl(KA), -0.5, 1.0, ALU.mult, ALU.add)
                    ts(drv[:, l, NKK:NKK + 8], pl(KK), -1.0, None, ALU.mult)
                    tt(drv[:, l, KK2:KK2 + 8], pl(KK), pl(KK), ALU.mult).then_inc(drv_ready, 1)
                dve.wait_ge(drv_ready, DEPTH)
                dve.wait_ge(clears, 1)
                dve.wait_ge(e["x_free"], 1)

            for l in range(DEPTH):
                x_norm(2 * l, l, gain(l, 0))
                k, t = start[l, "lora"]
                splits(k, 0)
                sums(t, 2 * (1 - l), lambda b: zt[:, 3 + b, 1:])
                if l:
                    k, t = start[l, "vres"]
                    lo(k + LEAD)
                    sums(t, 2, lambda b: zt[:, 5, 1:], 1)
                if l == 0:
                    parameters()
                t_all = start[l, "pairs"][1]
                dve.wait_ge(tile_out, t_all)
                for j in range(2 + l):
                    rows = slice(0, P if j < 2 else VRES)
                    tt(lact[rows, j, :], zt[rows, 3 + j, 0:SEQ], zt[rows, 3 + j, 1:], ALU.subtract).then_inc(l_diff, 1)
                    dve.wait_ge(l_diff, 2 * l + j + 1)
                    mu = prm[rows, l, MU + 24 + j:MU + 25 + j]
                    stt(lact[rows, j, :], lact[rows, j, :], mu, zt[rows, 3 + j, 1:], ALU.mult,
                        ALU.add).then_inc(l_shift, 1)
                dve.wait_ge(l_tanh, 2 * l + 2)
                ts(lact[:, 1, :], lact[:, 1, :], 0.5, 0.5, ALU.mult, ALU.add).then_inc(l_ready, 1)
                k, t = start[l, "pairs"]

                def place(g):
                    return lambda b: zt[:, 2 * g + b, 1:]
                splits(k, 0)
                sums(t, 0, place(0))
                for j in range(2):
                    lo(k + 4 + LEAD + j)

                def turn(i):
                    def finish(g):
                        sums(t + 4 + 2 * g + i * 6, (2, 2, 0)[g + 1], place((1, 2, 0)[g + 1]))

                    def step(j):
                        if j == 0:
                            dve.wait_ge(lo_done, k + 8 + LEAD + i * 12)
                        lo(k + 8 + j + LEAD, i * 3)
                    mixer(l, i, PAIRS * l + i, t + 4 + i * 6, step, finish)
                key_norms(l, 0, PAIRS * l)
                loop(dve, PAIRS - 1, turn)

                def finish(g):
                    if g < 1:
                        sums(t + 46 + 2 * g, 2, place(g + 2))

                def step(j):
                    if j == 0:
                        dve.wait_ge(lo_done, k + 92 + LEAD)
                    if j < 10:
                        lo(k + 92 + j + LEAD)
                mixer(l, PAIRS - 1, PAIRS * l + PAIRS - 1, t + 46, step, finish, False)
                k, t = start[l, "out"]
                hidden = lambda a: lambda b: yo[:, bass.ds(a + b, 1), :].rearrange("p a b -> p (a b)")
                for g in range(2):
                    lo(k + 6 + g + LEAD)
                    sums(t + 2 * g, 2 * g, lambda b: yo[:, 2 * g + b, :])

                def turn(i):
                    for g in range(2):
                        splits(k + 8 + 4 * g, i * 2)
                        sums(t + 4 + 2 * g + i * 4, 2 * g, hidden(i * 4 + 4 + 2 * g))
                loop(dve, 3, turn)
                y_norm(2 * l, gain(l, 1))
                x_norm(2 * l + 1, l, gain(l, 2))
                k, t = start[l, "mlp"]
                for q0, nq, last in runs(l):
                    def quarter(q):
                        qq = q + q0

                        def up_turn(i):
                            for g in range(2):
                                splits(k + 4 * g, qq * 16 + i * 2)
                                T = t + 2 * g + qq * 32 + i * 4
                                M = 64 * l + 2 * g + qq * 16 + i * 4
                                hid = lambda b: AR[:, b, :, :].rearrange("p a b -> p (a b)")
                                for b in range(2):
                                    dve.wait_ge(half_out, T + b + 1)
                                    tt(hid(b), bank[2 * g + b][:, 0:SEQ], xl[:, b, :], ALU.add).then_inc(up_sum, 1)
                                for b in range(2):
                                    dve.wait_ge(up_sum, M + b + 1)
                                    stt(hid(b), hid(b), 0.0, hid(b), ALU.max, ALU.mult).then_inc(up_relu, 1)
                                for b in range(2):
                                    dve.wait_ge(up_hi, M + b + 1)
                                    at = bass.ds(i * 4 + 2 * g + b, 1)
                                    tt(mT[:, at, 1, :], hid(b).unsqueeze(1), mT[:, at, 0, :].bitcast(F32),
                                       ALU.subtract).then_inc(tile_out, 1)
                        loop(dve, 4, up_turn)

                        def down_turn(i):
                            for g in range(2):
                                splits(k + 32 + 4 * g, qq * 16 + i * 2)
                                T = t + 16 + 2 * g + qq * 32 + i * 4
                                M = 64 * l + 2 * g + qq * 16 + i * 4
                                for b in range(2):
                                    dve.wait_ge(half_out, T + b + 1)
                                    tt(xl[:, b, :], bank[2 * g + b][:, 0:SEQ], xl[:, b, :],
                                       ALU.add).then_inc(down_sum, 1)
                                for b in range(2):
                                    dve.wait_ge(down_sum, M + b + 1)
                                    at = bass.ds(i * 4 + 2 * g + b, 1)
                                    tt(yo[:, at, :], yo[:, at, :], xl[:, b, :].unsqueeze(1),
                                       ALU.add).then_inc(tile_out, 1)
                        dve.wait_ge(clears, 2 + l)
                        loop(dve, 3 if last else 4, down_turn)
                        if last:
                            down_turn(3)
                    loop(dve, nq, quarter)
                y_norm(2 * l + 1, gain(l, 3))


_INS = ["x", "norm_mix_pre", "norm_mix_post", "norm_mlp_pre", "norm_mlp_post", "w_in", "w_in_vres", "shift_mu",
        "shift_mu_vres", "decay_w0", "decay_w2", "iclr_a0", "iclr_a2", "vres_v0", "vres_v2", "gate_g2", "k_k", "k_a",
        "r_k", "lnx_gain", "lnx_bias", "w_out", "w_up", "w_down"]


def kernel(**inputs):
    import concourse.bacc as bacc
    from concourse.bass_utils import run_bass_kernel_spmd

    nc = bacc.Bacc("TRN2", target_bir_lowering=False, num_devices=1)
    consts, levels = shape_constants()
    arrays = {"in_consts": consts, "in_levels": levels}
    for name in _INS:
        arrays["in_" + name] = np.ascontiguousarray(inputs[name])
    args = [nc.dram_tensor(name, a.shape, mybir.dt.from_np(a.dtype), kind="ExternalInput").ap()
            for name, a in arrays.items()]
    out = nc.dram_tensor("out_0", (1, SEQ, D), F32, kind="ExternalOutput").ap()
    trunk(nc, *args, out)
    r = run_bass_kernel_spmd(nc, [arrays], core_ids=[0])
    return r.results[0]["out_0"]
```
